# Optimizing a Trainium2 kernel written in Bass

```python
import math
import jax, jax.numpy as jnp
from jax import lax
import numpy as np

D_MODEL = 1024
BATCH = 1
SEQ = 512
DEPTH = 2

N_A = DEPTH // 2
N_B = DEPTH - N_A
CONV_WIDTH = 3
N_HEADS = 8
HEAD_DIM = 64
V_DIM = 2 * HEAD_DIM
D_FF = 4 * D_MODEL
Q_BLOCK = 128
EPS = 1e-6
NEG_INF = -1e30

kernel_name = "yoco_shortconv_diffattn_trunk"

def rms_norm(x, g):
    xf = x.astype(jnp.float32)
    y = xf * lax.rsqrt(jnp.mean(xf * xf, axis=-1, keepdims=True) + EPS)
    return (y * g.astype(jnp.float32)).astype(x.dtype)

def lambda_init_fn(layer_idx):
    return 0.8 - 0.6 * math.exp(-0.3 * layer_idx)

def short_conv_mixer(h, w_in, conv_w, w_out):
    bcv = h @ w_in
    b_gate, c_gate, v = jnp.split(bcv, 3, axis=-1)
    u = c_gate * v
    u = lax.conv_general_dilated(
        u, conv_w[:, None, :].astype(u.dtype),
        window_strides=(1,), padding=[(CONV_WIDTH - 1, 0)],
        dimension_numbers=("NWC", "WIO", "NWC"),
        feature_group_count=D_MODEL)
    return (b_gate * u) @ w_out

def squared_relu_mlp(h, w_up, w_down):
    a = jax.nn.relu(h @ w_up)
    return (a * a) @ w_down

def shared_kv(x, kv_norm, w_kv, k_norm):
    b, s, _ = x.shape
    kv = rms_norm(x, kv_norm) @ w_kv
    k = kv[..., :N_HEADS * 2 * HEAD_DIM].reshape(b, s, N_HEADS, 2, HEAD_DIM)
    k = rms_norm(k, k_norm)
    v = kv[..., N_HEADS * 2 * HEAD_DIM:].reshape(b, s, N_HEADS, V_DIM)
    return k, v

def diff_attention(h, k, v, w_q, q_norm, lq1, lk1, lq2, lk2, sub_norm, w_o, lam_init):
    b, s, _ = h.shape
    q = (h @ w_q).reshape(b, s, N_HEADS, 2, HEAD_DIM)
    q = rms_norm(q, q_norm)
    lam = (jnp.exp(jnp.sum(lq1.astype(jnp.float32) * lk1.astype(jnp.float32)))
           - jnp.exp(jnp.sum(lq2.astype(jnp.float32) * lk2.astype(jnp.float32)))
           + lam_init)
    scale = HEAD_DIM ** -0.5
    outs = []
    for i in range(s // Q_BLOCK):
        q_end = (i + 1) * Q_BLOCK
        qb = q[:, i * Q_BLOCK:q_end]
        kb = k[:, :q_end]
        vb = v[:, :q_end]
        sc = jnp.einsum('bqhcd,bkhcd->bhcqk', qb, kb,
                        preferred_element_type=jnp.float32) * scale
        q_pos = i * Q_BLOCK + jnp.arange(Q_BLOCK)
        k_pos = jnp.arange(q_end)
        causal = k_pos[None, :] <= q_pos[:, None]
        p = jax.nn.softmax(jnp.where(causal, sc, NEG_INF), axis=-1)
        a = p[:, :, 0] - lam * p[:, :, 1]
        outs.append(jnp.einsum('bhqk,bkhe->bqhe', a.astype(vb.dtype), vb))
    o = jnp.concatenate(outs, axis=1)
    o = rms_norm(o, sub_norm) * (1.0 - lam_init)
    return o.reshape(b, s, N_HEADS * V_DIM) @ w_o

def setup_inputs(seed: int = 0) -> dict:
    key = jax.random.key(seed)
    ks = jax.random.split(key, 24)
    f32 = jnp.float32

    def nrm(k, shape, scale):
        return jax.random.normal(k, shape, f32) * scale

    def gain(k, shape):
        return 1.0 + 0.02 * jax.random.normal(k, shape, f32)

    D = D_MODEL
    return {
        "x": jax.random.normal(ks[0], (BATCH, SEQ, D), f32),
        "a_norm": gain(ks[1], (N_A, D)),
        "a_w_in": nrm(ks[2], (N_A, D, 3 * D), D ** -0.5),
        "a_conv": nrm(ks[3], (N_A, CONV_WIDTH, D), CONV_WIDTH ** -0.5),
        "a_w_out": nrm(ks[4], (N_A, D, D), D ** -0.5),
        "kv_norm": gain(ks[5], (D,)),
        "w_kv": nrm(ks[6], (D, N_HEADS * 2 * HEAD_DIM + N_HEADS * V_DIM), D ** -0.5),
        "k_norm": gain(ks[7], (HEAD_DIM,)),
        "b_norm": gain(ks[8], (N_B, D)),
        "w_q": nrm(ks[9], (N_B, D, N_HEADS * 2 * HEAD_DIM), D ** -0.5),
        "q_norm": gain(ks[10], (N_B, HEAD_DIM)),
        "lam_q1": nrm(ks[11], (N_B, HEAD_DIM), 0.1),
        "lam_k1": nrm(ks[12], (N_B, HEAD_DIM), 0.1),
        "lam_q2": nrm(ks[13], (N_B, HEAD_DIM), 0.1),
        "lam_k2": nrm(ks[14], (N_B, HEAD_DIM), 0.1),
        "sub_norm": gain(ks[15], (N_B, V_DIM)),
        "w_o": nrm(ks[16], (N_B, N_HEADS * V_DIM, D), (N_HEADS * V_DIM) ** -0.5),
        "mlp_norm": gain(ks[17], (DEPTH, D)),
        "w_up": nrm(ks[18], (DEPTH, D, D_FF), D ** -0.5),
        "w_down": nrm(ks[19], (DEPTH, D_FF, D), D_FF ** -0.5),
    }

def reference(x, a_norm, a_w_in, a_conv, a_w_out, kv_norm, w_kv, k_norm,
              b_norm, w_q, q_norm, lam_q1, lam_k1, lam_q2, lam_k2, sub_norm,
              w_o, mlp_norm, w_up, w_down):
    k_sh = None
    v_sh = None
    for l in range(DEPTH):
        if l < N_A:
            x = x + short_conv_mixer(rms_norm(x, a_norm[l]), a_w_in[l],
                                     a_conv[l], a_w_out[l])
        else:
            j = l - N_A
            x = x + diff_attention(rms_norm(x, b_norm[j]), k_sh, v_sh, w_q[j],
                                   q_norm[j], lam_q1[j], lam_k1[j], lam_q2[j],
                                   lam_k2[j], sub_norm[j], w_o[j],
                                   lambda_init_fn(l))
        x = x + squared_relu_mlp(rms_norm(x, mlp_norm[l]), w_up[l], w_down[l])
        if l == N_A - 1:
            k_sh, v_sh = shared_kv(x, kv_norm, w_kv, k_norm)
    return x


_drawn_inputs = setup_inputs


def setup_inputs(seed=0):
    import zlib

    import numpy as np

    out = dict(_drawn_inputs(seed))
    spreads = {}
    factors = {'kv_norm': 6.849,
     'k_norm': 8.0,
     'b_norm': 8.0,
     'q_norm': 8.0,
     'lam_k1': 3.357,
     'lam_q2': 3.85,
     'lam_k2': 5.641,
     'sub_norm': 8.0,
     'mlp_norm': 2.83}
    for name, (base, spread) in spreads.items():
        noise = np.random.default_rng([zlib.crc32(name.encode()), seed]).standard_normal(out[name].shape)
        drawn = base * np.exp(spread * noise) if base else spread * noise
        out[name] = __import__('jax').numpy.asarray(drawn.astype(out[name].dtype))
    for name, factor in factors.items():
        out[name] = (out[name] * factor).astype(out[name].dtype)
    return out
```

```python
import math
from contextlib import ExitStack

import concourse.bass as bass
from concourse import mybir


F32 = mybir.dt.float32
F32R = mybir.dt.float32r
BF16 = mybir.dt.bfloat16
ALU = mybir.AluOpType
ACT = mybir.ActivationFunctionType
AX_X = mybir.AxisListType.X

P = 128
T = 512
TB = T // P
D = 1024
KC = D // P
F = 4 * D
NQ = 4
H = 8
HD = 64
EPS = 1e-6
NEG = -1e30
LAM_INIT = 0.8 - 0.6 * math.exp(-0.3 * 1)
SLAB = 1024

RAW = 2
RING = 4
AHEAD = 2
ACC = 4
BC, STAT = 6, 7
B_Q, B_AT, B_O, B_BC = 4, 5, 6, 7

N_IN, N_OUT = 24, 8
S_IN = 0
S_OUT = S_IN + N_IN
S_MLP0 = S_OUT + N_OUT
S_V = S_MLP0 + NQ * 16
S_K = S_V + 8
S_Q = S_K + 8
S_WO = S_Q + H
S_MLP1 = S_WO + 8
S_END = S_MLP1 + NQ * 16

U_IN, U_OUT, U_MLP0, U_V, U_K, U_WO, U_MLP1 = 0, 24, 32, 96, 104, 112, 120

I_A, I_Z, I_M0, I_KV, I_Q, I_O, I_M1 = range(7)
NORM_A, NORM_M0, NORM_B, NORM_M1 = range(4)


def slot(n):
    return (n % 2) if S_Q <= n < S_WO else n % RING


def freed(n):
    if n >= S_WO and n < S_WO + 2:
        return n - 1
    if S_Q + 2 <= n < S_WO:
        return n - 1
    return n - RING + 1 if n >= RING else 0


def at_start(i):
    return isinstance(i, int) and i == 0


def build(nc, x, a_norm, a_w_in, a_conv, a_w_out, kv_norm, w_kv, k_norm, b_norm, w_q, q_norm,
          lam_q1, lam_k1, lam_q2, lam_k2, sub_norm, w_o, mlp_norm, w_up, w_down, out):
    with ExitStack() as ctx:
        def sb(name, shape, dt=F32):
            return ctx.enter_context(nc.sbuf_tensor(name, shape, dt))

        def sem(name):
            return ctx.enter_context(nc.semaphore(name))

        xT = sb("xT", [P, KC, T])
        h1 = sb("h1", [P, 2, KC, T], F32R)
        h2 = sb("h2", [P, 2, KC, T], F32R)
        ah = sb("ah", [P, 16, T], F32R)
        kv = sb("kv", [P, 16, T])
        w_raw = sb("w_raw", [P, RAW, SLAB])
        w_hi = sb("w_hi", [P, RING, SLAB], F32R)
        w_lo = sb("w_lo", [P, RING, SLAB], F32R)
        rB = sb("rB", [P, T])
        work = sb("work", [P, 4096])
        sqsum = work[:, 3584:4096]
        ident = sb("ident", [P, P])
        identb = sb("identb", [P, P], BF16)
        maskb = sb("maskb", [P, P], BF16)
        comp2 = sb("comp2", [P, 2])
        ones2 = sb("ones2", [P, 2])
        mhalf = sb("mhalf", [P, 8])
        gains = sb("gains", [P, 5, KC])
        conv = sb("conv", [P, 3, KC])
        hg = sb("hg", [P, 3])
        hgs = sb("hgs", [P, 3])
        lamv = sb("lamv", [P, 4, HD])
        lamp = sb("lamp", [P, HD])
        lams = sb("lams", [P, 8])
        nms = sb("nms", [P, 4, TB])
        rcol = sb("rcol", [P, 4, TB])
        r2 = sb("r2", [P, TB])
        qms = sb("qms", [P, 2, 8])
        qpw = sb("qpw", [P, 8])
        oms = sb("oms", [P, 8])
        ors = sb("ors", [P, 8])
        nmax = sb("nmax", [P, 2, 2])
        rsum = sb("rsum", [P, 2, 2])
        rinv = sb("rinv", [P, 2, 2])
        lrin = sb("lrin", [P, 2])
        ps = ctx.enter_context(nc.psum_tensor("ps", [P, 8, T], F32))

        g_a, g_m0, g_m1, g_kv, g_b = range(5)
        mix = [work[:, i * T:(i + 1) * T] for i in range(7)]
        U0 = 2 * T
        sqb = [work[:, 6 * T - 1024 + i * T:6 * T - 1024 + (i + 1) * T] for i in range(2)]
        p_buf = [work[:, (4 + 2 * i) * T:(6 + 2 * i) * T].rearrange("p (c k) -> p c k", c=2) for i in range(2)]
        at_hi = [ah[:, 0, :].rearrange("p (j q) -> p j q", j=2), ah[:, 2:4, :].rearrange("p a (j q) -> p (a j) q", j=2)]
        at_lo = [ah[:, 1, :].rearrange("p (j q) -> p j q", j=2), ah[:, 4:6, :].rearrange("p a (j q) -> p (a j) q", j=2)]
        q_hi, q_lo = [ah[:, 6 + 2 * b, :] for b in range(2)], [ah[:, 7 + 2 * b, :] for b in range(2)]
        k_hi, k_lo = [ah[:, 10 + 2 * b, :] for b in range(2)], [ah[:, 11 + 2 * b, :] for b in range(2)]
        v_hi, v_lo = ah[:, 14, :].rearrange("p (t e) -> p t e", t=TB), ah[:, 15, :].rearrange("p (t e) -> p t e", t=TB)
        v_all = kv[:, 8:16, :].rearrange("p a b -> p (a b)").rearrange("p (t f) -> p t f", t=TB)
        x_tok = kv[:, 0:8, :].rearrange("p a b -> p (a b)").rearrange("p (t f) -> p t f", t=TB)
        raw_qk = [work[:, 0:T], work[:, 2 * T:3 * T]]
        sq_qk = [work[:, T:2 * T], work[:, 3 * T:4 * T]]
        o_sb, o_sq = work[:, 2 * T:3 * T], work[:, 3 * T:4 * T]
        h_of = [h1, h2, h1, h2, h1, h2, h1]

        s_x = sem("s_x")
        s_par = sem("s_par")
        s_raw = [sem(f"s_raw{i}") for i in range(RAW)]
        s_whi = sem("s_whi")
        s_wlo = sem("s_wlo")
        s_used = sem("s_used")
        s_acc = sem("s_acc")
        s_zero = sem("s_zero")
        s_cst = sem("s_cst")
        s_xt = sem("s_xt")
        s_xd = sem("s_xd")
        s_xa = sem("s_xa")
        s_hi = sem("s_hi")
        s_lo = sem("s_lo")
        s_sq = sem("s_sq")
        s_add = sem("s_add")
        s_nst = sem("s_nst")
        s_nms = sem("s_nms")
        s_nrc = sem("s_nrc")
        s_nbc = sem("s_nbc")
        s_rB = sem("s_rB")
        s_mix = sem("s_mix")
        s_r = sem("s_r")
        s_ahi = sem("s_ahi")
        s_alo = sem("s_alo")
        s_lam = sem("s_lam")
        s_qc = sem("s_qc")
        s_qsq = sem("s_qsq")
        s_qst = sem("s_qst")
        s_qms = sem("s_qms")
        s_qrs = sem("s_qrs")
        s_qbc = sem("s_qbc")
        s_qn = sem("s_qn")
        s_qhi = sem("s_qhi")
        s_qlo = sem("s_qlo")
        s_vhi = sem("s_vhi")
        s_vlo = sem("s_vlo")
        s_S = sem("s_S")
        s_mx = sem("s_mx")
        s_exp = sem("s_exp")
        s_sc = sem("s_sc")
        s_at = sem("s_at")
        s_T = sem("s_T")
        s_Thi = sem("s_Thi")
        s_Tlo = sem("s_Tlo")
        s_pv = sem("s_pv")
        s_oc = sem("s_oc")
        s_ost = sem("s_ost")
        s_oms = sem("s_oms")
        s_ors = sem("s_ors")
        s_obc = sem("s_obc")
        s_on = sem("s_on")
        s_fT = sem("s_fT")
        s_fc = sem("s_fc")
        s_out = sem("s_out")

        win_d = a_w_in.rearrange("l (k p) c -> p (l k) c", p=P)
        wout_d = a_w_out.rearrange("l (k p) c -> p (l k) c", p=P)
        wkv_d = w_kv.rearrange("(k p) c -> p k c", p=P)
        wq_d = w_q.rearrange("l (k p) c -> p (l k) c", p=P)
        wo_d = w_o.rearrange("l (k p) c -> p (l k) c", p=P)
        up_d = [w_up[l].rearrange("(k p) c -> p k c", p=P) for l in range(2)]
        dn_d = [w_down[l].rearrange("(k p) c -> p k c", p=P) for l in range(2)]
        out_d = out.rearrange("b (t p) d -> p (b t) d", p=P)
        x_d = x.rearrange("b (t p) d -> p (b t) d", p=P)

        block = ctx.enter_context(nc.Block())

        @block.sync
        def _(sp):
            def load(n, src, off=0):
                if n >= RAW:
                    sp.wait_ge(s_wlo, off + n - RAW + 1)
                dst = w_raw[:, n % RAW, :].rearrange("p (k c) -> p k c", k=src.shape[1])
                sp.dma_start(dst, src).then_inc(s_raw[n % RAW], 16)

            for t in range(TB):
                sp.dma_start(x_tok[:, t, :], x_d[:, t, :]).then_inc(s_x, 16)

            def cols(w, c):
                return w[:, :, c * P:(c + 1) * P]

            for j in range(KC):
                for i, part in enumerate((1, 2, 0)):
                    load(S_IN + 3 * j + i, cols(win_d, part * KC + j))
            for m in range(KC):
                load(S_OUT + m, cols(wout_d, m))

            def mlp(layer, base):
                with sp.Fori(0, NQ) as q:
                    for j in range(8):
                        load(base + j, up_d[layer][:, :, bass.ds(q * D + j * P, P)], q * 16)
                    for m in range(8):
                        load(base + 8 + m, dn_d[layer][:, bass.ds(q * KC, KC), m * P:(m + 1) * P], q * 16)

            mlp(0, S_MLP0)
            for n in range(8):
                g, kk = n // 4, n % 4
                load(S_V + n, wkv_d[:, 2 * kk:2 * kk + 2, D + g * T:D + (g + 1) * T])
            for h in range(H):
                load(S_K + h, cols(wkv_d, h))
            for h in range(H):
                load(S_Q + h, cols(wq_d, h))
            for m in range(KC):
                load(S_WO + m, cols(wo_d, m))
            mlp(1, S_MLP1)
            for m in range(KC):
                sp.wait_ge(s_fc, m + 1)
                sp.dma_start(out_d[:, :, m * P:(m + 1) * P],
                             kv[:, m, :].rearrange("p (t c) -> p t c", t=TB)).then_inc(s_out, 16)
            sp.wait_ge(s_out, 16 * KC)

        @block.gpsimd
        def _(pool):
            with nc.allow_non_contiguous_dma(reason="gains: one float a feature"):
                def par(dst, src):
                    pool.dma_start(dst, src).then_inc(s_par, 16)
                par(gains[:, g_a, :], a_norm.rearrange("l (k p) -> p (l k)", p=P))
                par(gains[:, g_m0:g_m1 + 1, :], mlp_norm.rearrange("l (k p) -> p l k", p=P))
                par(gains[:, g_kv, :], kv_norm.rearrange("(k p) -> p k", p=P))
                par(gains[:, g_b, :], b_norm.rearrange("l (k p) -> p (l k)", p=P))
                par(conv[:, :, :], a_conv.rearrange("l w (k p) -> p (l w) k", p=P))
                for c in range(2):
                    par(hg[c * HD:(c + 1) * HD, 0:1], q_norm.rearrange("l d -> d l"))
                    par(hg[c * HD:(c + 1) * HD, 1:2], k_norm.rearrange("(d o) -> d o", o=1))
                par(hg[:, 2:3], sub_norm.rearrange("l d -> d l"))
                for i, v in enumerate((lam_q1, lam_k1, lam_q2, lam_k2)):
                    par(lamv[:, i, :], v.to_broadcast([P, HD]))
            nc.gpsimd.memset(ident[:], 0.0).then_inc(s_zero, 1)
            nc.gpsimd.memset(maskb[:], 0.0).then_inc(s_zero, 1)
            pool.wait_ge(s_zero, 2)
            nc.gpsimd.affine_select(out=ident[:], in_=ident[:], compare_op=ALU.not_equal, fill=1.0, base=0,
                                    pattern=[[-1, P]], channel_multiplier=1).then_inc(s_zero, 1)
            nc.gpsimd.affine_select(out=maskb[:], in_=maskb[:], compare_op=ALU.is_ge, fill=NEG, base=0,
                                    pattern=[[-1, P]], channel_multiplier=1).then_inc(s_zero, 1)
            nc.gpsimd.memset(mhalf[:], -0.5).then_inc(s_zero, 1)
            zero = [(t, b, j) for t in (at_hi, at_lo) for b, j in ((0, 1), (1, 3))]

            def norm(i):
                if i > 0:
                    pool.wait_ge(s_nst, i)
                nc.gpsimd.memset(sqsum, 0.0).then_inc(s_zero, 1)
                pool.wait_ge(s_zero, 6 + i + (4 if i == NORM_M1 else 0))
                for m in range(KC):
                    pool.wait_ge(s_sq, 8 * i + m + 1)
                    nc.gpsimd.tensor_tensor(sqsum, sqsum, sqb[m % 2], ALU.add).then_inc(s_add, 1)
                    pool.wait_ge(s_add, 8 * i + m + 1)
                pool.wait_ge(s_nms, i + 1)
                nc.gpsimd.tensor_tensor(rcol[:, i, :], nms[:, i, :], mhalf[:, 0:TB], ALU.pow).then_inc(s_nrc, 1)

            norm(NORM_A)
            norm(NORM_M0)
            norm(NORM_B)

            def head_scale(i, b, sq):
                pool.wait_ge(s_qms, i * 2 + 2)
                nc.gpsimd.tensor_tensor(qpw[:], qms[:, b, :], mhalf[:], ALU.pow).then_inc(s_qrs, 1)
                pool.wait_ge(s_qrs, i * 2 + 1)
                nc.gpsimd.tensor_tensor(sq.rearrange("p (t c d) -> p t c d", t=TB, c=2),
                                        qpw[:].rearrange("p (t c) -> p t c", c=2).unsqueeze(3).to_broadcast([P, TB, 2, HD]),
                                        rcol[:, NORM_B, :].unsqueeze(2).unsqueeze(3).to_broadcast([P, TB, 2, HD]),
                                        ALU.mult).then_inc(s_qrs, 1)

            def out_scale(h):
                pool.wait_ge(s_oms, h + 1)
                nc.gpsimd.tensor_tensor(ors[:], oms[:], mhalf[:], ALU.pow).then_inc(s_ors, 1)

            pool.wait_ge(s_alo, 32)
            pool.wait_ge(s_used, S_V)
            for t, b, j in zero:
                nc.gpsimd.memset(t[b][:, j, 0:P].bitcast(F32), 0.0).then_inc(s_zero, 1)
            for i in range(H + 1):
                head_scale(i, i % 2, sq_qk[i % 2])
            head_scale(H + 1, (H + 1) % 2, sq_qk[0])
            with pool.Fori(0, (H - 2) // 2) as it:
                for e in range(2):
                    out_scale(it * 2 + e)
                    head_scale(it * 2 + (H + 2 + e), e, sq_qk[0])
            out_scale(H - 2)
            out_scale(H - 1)
            norm(NORM_M1)

        @block.tensor
        def _(pe):
            def wait_slab(n, off=0):
                pe.wait_ge(s_wlo, off + n + 1)

            def wait_acc(u, off=0):
                if u >= ACC:
                    pe.wait_ge(s_acc, off + u - ACC + 1)

            def product(bank, n, src, ks, wait_chunk=None, ks0=0, total=KC):
                s = slot(n)
                for k in ks:
                    if wait_chunk is not None:
                        wait_chunk(k)
                    for i, (w, half) in enumerate(((w_hi, 0), (w_hi, 1), (w_lo, 0))):
                        last = nc.tensor.matmul(ps[:, bank, :], w[:, s, k * P:(k + 1) * P], src(half, k),
                                                start=(k == 0 and i == 0), stop=(k == total - 1 and i == 2))
                return last

            def operand(i):
                return lambda half, k: h_of[i][:, half, k, :]

            def chunks_of(i):
                return lambda k: pe.wait_ge(s_lo, 8 * i + k + 1)

            def dense(n, u, i, first=False):
                wait_acc(u)
                wait_slab(n)
                product(u % ACC, n, operand(i), range(KC), chunks_of(i) if first else None).then_inc(s_used, 1)

            def norm_sums(i):
                pe.wait_ge(s_add, 8 * (i + 1))
                for t in range(TB):
                    last = nc.tensor.matmul(ps[:, STAT, 2 * t:2 * t + 2], sqsum[:, t * P:(t + 1) * P], ones2[:],
                                            start=True, stop=True)
                last.then_inc(s_nst, 1)

            def spread(bank, col, done, times=P):
                for t in range(TB):
                    last = nc.tensor.matmul(ps[:, bank, t * P:(t + 1) * P], col(t), ident[:], start=True, stop=True)
                last.then_inc(done, 1)

            def norm_spread(i):
                pe.wait_ge(s_nrc, i + 1)
                spread(BC, lambda t: rcol[:, i, t:t + 1].to_broadcast([P, P]), s_nbc)

            pe.wait_ge(s_zero, 5)
            pe.wait_ge(s_cst, 5)
            for t in range(TB):
                pe.wait_ge(s_x, 16 * TB)
                for hf in range(2):
                    for k in range(4):
                        c = (4 * hf + k) * P
                        last = nc.tensor.transpose(ps[:, 2 * t + hf, k * P:(k + 1) * P], x_tok[:, t, c:c + P], ident[:])
                    last.then_inc(s_xt, 1)
            pe.wait_ge(s_xd, TB)
            pe.wait_ge(s_xa, TB)

            for n in range(N_IN):
                dense(S_IN + n, U_IN + n, I_A, n == 0)
                if n == 0:
                    norm_sums(NORM_A)
                if n == 1:
                    norm_spread(NORM_A)
            for m in range(KC):
                dense(S_OUT + m, U_OUT + m, I_Z, m == 0)

            def mlp(layer, base, ubase, inp, norm):
                def quarter(q, first=False, last=False):
                    for j in range(8):
                        wait_acc(ubase + j, q * 16)
                        wait_slab(base + j, q * 16)
                        product((ubase + j) % ACC, base + j, operand(inp), range(KC),
                                chunks_of(inp) if first and j == 0 else None).then_inc(s_used, 1)
                        if first and j == 0:
                            norm_sums(norm)
                        if first and j == 1:
                            norm_spread(norm)
                    for m in range(8):
                        wait_acc(ubase + 8 + m, q * 16)
                        wait_slab(base + 8 + m, q * 16)

                        def act_chunk(k):
                            pe.wait_ge(s_alo, q * 8 + (32 * layer + k + 1))
                        product((ubase + m) % ACC, base + 8 + m, lambda half, k: ah[:, 8 * half + k, :],
                                range(KC), act_chunk if m == 0 else None).then_inc(s_used, 1)
                        if last and layer == 1 and m >= 1:
                            final(m - 1)
                    if last and layer == 1:
                        final(KC - 1)

                quarter(0, first=True)
                with pe.Fori(1, NQ - 1) as q:
                    quarter(q)
                quarter(NQ - 1, last=True)

            def final(m):
                pe.wait_ge(s_acc, U_MLP1 + 16 * (NQ - 1) + 8 + m + 1)
                if m >= 2:
                    pe.wait_ge(s_fc, m - 1)
                for t in range(TB):
                    last = nc.tensor.transpose(ps[:, BC + m % 2, t * P:(t + 1) * P], xT[:, m, t * P:(t + 1) * P], ident[:])
                last.then_inc(s_fT, 1)

            mlp(0, S_MLP0, U_MLP0, I_M0, NORM_M0)

            for g in range(2):
                for kk in range(4):
                    n = S_V + 4 * g + kk
                    wait_slab(n)
                    s = slot(n)
                    for t in range(TB):
                        if kk == 0:
                            wait_acc(U_V + 4 * g + t)
                        for k2 in range(2):
                            k = 2 * kk + k2
                            if g == 0 and t == 0:
                                pe.wait_ge(s_lo, 8 * I_KV + k + 1)
                            for i, (half, w) in enumerate(((0, w_hi), (0, w_lo), (1, w_hi))):
                                last = nc.tensor.matmul(ps[:, (U_V + t) % ACC, :], h2[:, half, k, t * P:(t + 1) * P],
                                                        w[:, s, k2 * T:(k2 + 1) * T],
                                                        start=(k == 0 and i == 0), stop=(k == KC - 1 and i == 2))
                    last.then_inc(s_used, 1)
                    if g == 0 and kk == 0:
                        norm_sums(NORM_B)

            def head_sums(i, sq, bank, at):
                pe.wait_ge(s_qsq, i + 1)
                if not at_start(i):
                    pe.wait_ge(s_qms, i * 2)
                for t in range(TB):
                    last = nc.tensor.matmul(ps[:, bank, at + 2 * t:at + 2 * t + 2], sq[:, t * P:(t + 1) * P], comp2[:],
                                            start=True, stop=True)
                last.then_inc(s_qst, 1)

            def head_spread(i, sq, bank):
                pe.wait_ge(s_qrs, i * 2 + 2)
                if not at_start(i):
                    pe.wait_ge(s_qn, i)
                spread(bank, lambda t: sq[:, t * P:(t + 1) * P], s_qbc)

            for h in range(H):
                wait_acc(U_K + h)
                wait_slab(S_K + h)
                product((U_K + h) % ACC, S_K + h, operand(I_KV), range(0, 4))
                if h >= 1:
                    head_sums(h - 1, sq_qk[(h - 1) % 2], STAT, 0)
                product((U_K + h) % ACC, S_K + h, operand(I_KV), range(4, KC)).then_inc(s_used, 1)
                if h >= 1:
                    head_spread(h - 1, sq_qk[(h - 1) % 2], BC)
            wait_slab(S_Q)
            product(B_Q, S_Q, operand(I_Q), range(0, 4), chunks_of(I_Q))
            head_sums(H - 1, sq_qk[1], STAT, 0)
            product(B_Q, S_Q, operand(I_Q), range(4, KC)).then_inc(s_used, 1)
            head_spread(H - 1, sq_qk[1], BC)
            head_sums(H, sq_qk[0], B_Q, 8)
            head_spread(H, sq_qk[0], B_BC)
            pe.wait_ge(s_acc, U_WO)

            def scores(h, i, b):
                if i == 0:
                    pe.wait_ge(s_qlo, h * 2 + 2)
                if not (at_start(h) and i < 2):
                    pe.wait_ge(s_exp, h * 8 + 2 * (i - 1))
                kw = max((i + 1) * P, 2 * P)
                for c in range(2):
                    rows = slice(c * HD, (c + 1) * HD)
                    bank = 2 * (i % 2) + c
                    for j, (q, k) in enumerate(((q_hi, k_hi), (q_hi, k_lo), (q_lo, k_hi))):
                        nc.tensor.matmul(ps[:, bank, 0:kw], q[b][rows, i * P:(i + 1) * P], k[b][rows, 0:kw],
                                         start=(j == 0), stop=False)
                    last = nc.tensor.matmul(ps[:, bank, i * P:(i + 1) * P], identb[:], maskb[:], start=False, stop=True)
                last.then_inc(s_S, 1)

            def weights_T(h, i):
                pe.wait_ge(s_at, h * 4 + i + 1)
                if not (at_start(h) and i == 0):
                    pe.wait_ge(s_Thi, h * 4 + i)
                    pe.wait_ge(s_Tlo, h * 4 + i)
                for j in range(i + 1):
                    last = nc.tensor.transpose(ps[:, B_AT, j * P:(j + 1) * P], p_buf[i % 2][:, 0, j * P:(j + 1) * P], ident[:])
                last.then_inc(s_T, 1)

            def values(h, p):
                pe.wait_ge(s_Thi, h * 4 + 2 * p + 2)
                pe.wait_ge(s_Tlo, h * 4 + 2 * p + 2)
                if p == 0:
                    pe.wait_ge(s_vlo, h + 1)
                    if not at_start(h):
                        pe.wait_ge(s_oc, h * 2)
                nj = 2 * p + 2
                for j in range(nj):
                    for i, (v, a) in enumerate(((v_hi, at_hi), (v_hi, at_lo), (v_lo, at_hi))):
                        last = nc.tensor.matmul(ps[:, B_O, p * 256:(p + 1) * 256], v[:, j, :], a[p][:, j, :],
                                                start=(j == 0 and i == 0), stop=(j == nj - 1 and i == 2))
                last.then_inc(s_pv, 1)

            def out_sums(h):
                pe.wait_ge(s_oc, h * 2 + 2)
                for t in range(TB):
                    last = nc.tensor.matmul(ps[:, B_Q, 2 * t:2 * t + 2], o_sq[:, t * P:(t + 1) * P], ones2[:],
                                            start=True, stop=True)
                last.then_inc(s_ost, 1)

            def out_spread(h):
                pe.wait_ge(s_ors, h + 1)
                spread(B_BC, lambda t: ors[:, 2 * t:2 * t + 1].to_broadcast([P, P]), s_obc)

            def head(h, b, prev, nxt):
                scores(h, 0, b)
                scores(h, 1, b)
                if prev is not None:
                    weights_T(prev, 3)
                if nxt is not None:
                    pe.wait_ge(s_wlo, nxt + (S_Q + 1))
                    pe.wait_ge(s_qms, nxt * 2 + 2 * H)
                    product(B_Q, S_Q + 1 - b, operand(I_Q), range(KC)).then_inc(s_used, 1)
                if prev is not None:
                    values(prev, 1)
                weights_T(h, 0)
                scores(h, 2, b)
                if nxt is not None:
                    pe.wait_ge(s_qc, nxt + (H + 1))
                    pe.wait_ge(s_qsq, nxt + (H + 1))
                if prev is not None:
                    out_sums(prev)
                if nxt is not None:
                    if prev is not None:
                        pe.wait_ge(s_oms, prev + 1)
                    head_sums(nxt + H, sq_qk[0], B_Q, 8)
                weights_T(h, 1)
                scores(h, 3, b)
                values(h, 0)
                if prev is not None:
                    pe.wait_ge(s_qn, h + (H + 1))
                    out_spread(prev)
                if nxt is not None:
                    if prev is not None:
                        pe.wait_ge(s_on, prev + 1)
                    head_spread(nxt + H, sq_qk[0], B_BC)
                weights_T(h, 2)

            head(0, 0, None, 1)
            with pe.Fori(0, (H - 2) // 2) as it:
                head(it * 2 + 1, 1, it * 2, it * 2 + 2)
                head(it * 2 + 2, 0, it * 2 + 1, it * 2 + 3)
            head(H - 1, 1, H - 2, None)
            weights_T(H - 1, 3)
            values(H - 1, 1)
            out_sums(H - 1)
            pe.wait_ge(s_on, H - 1)
            out_spread(H - 1)

            for m in range(KC):
                dense(S_WO + m, U_WO + m, I_O, m == 0)
            mlp(1, S_MLP1, U_MLP1, I_M1, NORM_M1)

        @block.scalar
        def _(act):
            def split(n, off=0):
                act.wait_ge(s_raw[n % RAW], off * (16 // RAW) + 16 * (n // RAW + 1))
                if freed(n):
                    act.wait_ge(s_used, off + freed(n))
                nc.scalar.activation(w_hi[:, slot(n), :], w_raw[:, n % RAW, :], ACT.Copy).then_inc(s_whi, 1)

            def chunk_hi(i, m, g):
                nc.scalar.activation(h_of[i][:, 0, m, :], xT[:, m, :], ACT.Copy, scale=gains[:, g, m:m + 1]).then_inc(s_hi, 1)

            def square(i, m):
                if 8 * i + m >= 2:
                    act.wait_ge(s_add, 8 * i + m - 1)
                nc.scalar.activation(sqb[m % 2], xT[:, m, :], ACT.Square).then_inc(s_sq, 1)

            def row_scales(count):
                act.wait_ge(s_nbc, count)
                nc.scalar.activation(rB[:], ps[:, BC, :], ACT.Copy).then_inc(s_rB, 1)

            for t in range(TB):
                act.wait_ge(s_xt, 2 * t + 2)
                nc.scalar.activation(xT[:, 4:8, t * P:(t + 1) * P],
                                     ps[:, 2 * t + 1, :].rearrange("p (k q) -> p k q", k=4), ACT.Copy).then_inc(s_xa, 1)
            act.wait_ge(s_par, 16 * 14)
            act.wait_ge(s_xd, TB)
            act.wait_ge(s_xa, TB)
            split(0)
            for m in range(KC):
                chunk_hi(I_A, m, g_a)
                square(NORM_A, m)
                if m == 3:
                    split(1)
            act.wait_ge(s_cst, 7)
            nc.scalar.activation(lams[:, 2:4], lams[:, 0:2], ACT.Exp).then_inc(s_lam, 1)
            for n in range(N_IN):
                split(n + AHEAD)
                if n == 1:
                    row_scales(1)
                if n % 3 == 2:
                    j = n // 3
                    act.wait_ge(s_mix, 9 * (j + 1))
                    nc.scalar.activation(h2[:, 0, j, :], mix[5 + j % 2], ACT.Copy).then_inc(s_hi, 1)
            for m in range(KC):
                split(S_OUT + m + AHEAD)
                act.wait_ge(s_acc, U_OUT + m + 1)
                chunk_hi(I_M0, m, g_m0)
                square(NORM_M0, m)

            def mlp(layer, base, ubase, count, after):
                def quarter(q, first=False, last=False):
                    for j in range(8):
                        split(base + j + AHEAD, q * 16)
                        if first and j == 0:
                            pass
                        if first and j == 1:
                            row_scales(count)
                        for jj in ((0, 1) if j == 1 else () if j == 0 else (j,)):
                            act.wait_ge(s_r, q * 8 + (32 * layer + jj + 1))
                            nc.scalar.activation(ah[:, jj, :], mix[jj % 2], ACT.Square).then_inc(s_ahi, 1)
                    for m in range(8):
                        n = base + 8 + m + AHEAD
                        if not (last and n + q * 16 >= S_END):
                            split(n, q * 16)
                        if last:
                            after(m)

                quarter(0, first=True)
                with act.Fori(1, NQ - 1) as q:
                    quarter(q)
                quarter(NQ - 1, last=True)

            def after0(m):
                act.wait_ge(s_acc, U_MLP0 + 56 + m + 1)
                chunk_hi(I_KV, m, g_kv)
                square(NORM_B, m)

            mlp(0, S_MLP0, U_MLP0, 2, after0)
            for n in range(8):
                split(S_V + n + AHEAD)
                chunk_hi(I_Q, n, g_b)
            def square_qk(i, src, sq, count):
                act.wait_ge(s_qc, count)
                if i >= 2:
                    act.wait_ge(s_qbc, i - 1)
                nc.scalar.activation(sq, src, ACT.Square).then_inc(s_qsq, 1)

            for h in range(H):
                split(S_K + h + AHEAD)
                square_qk(h, raw_qk[h % 2], sq_qk[h % 2], h + 1)

            def copy_q(h):
                act.wait_ge(s_used, h + (S_Q + 1))
                act.wait_ge(s_qhi, h * 2)
                act.wait_ge(s_qlo, h * 2)
                nc.scalar.activation(raw_qk[0], ps[:, B_Q, :], ACT.Copy).then_inc(s_qc, 1)
                act.wait_ge(s_qbc, h + H)
                nc.scalar.activation(sq_qk[0], ps[:, B_Q, :], ACT.Square).then_inc(s_qsq, 1)

            def split_qk(h, b):
                act.wait_ge(s_qn, h + (H + 1))
                nc.scalar.activation(q_hi[b], raw_qk[0], ACT.Copy).then_inc(s_qhi, 1)
                nc.scalar.activation(k_hi[b], kv[:, bass.ds(h, 1), :].rearrange("p a b -> p (a b)"), ACT.Copy).then_inc(s_qhi, 1)

            act.wait_ge(s_used, S_Q + 1)
            act.wait_ge(s_qn, 7)
            nc.scalar.activation(raw_qk[0], ps[:, B_Q, :], ACT.Copy).then_inc(s_qc, 1)
            act.wait_ge(s_qbc, 7)
            nc.scalar.activation(sq_qk[0], ps[:, B_Q, :], ACT.Square).then_inc(s_qsq, 1)
            act.wait_ge(s_used, S_V)
            split_qk(0, 0)

            def exps(h, i):
                act.wait_ge(s_mx, h * 4 + i + 1)
                if not (at_start(h) and i < 2):
                    act.wait_ge(s_T, h * 4 + i - 1)
                kw = (i + 1) * P
                for c in range(2):
                    nc.scalar.activation(p_buf[i % 2][:, c, 0:kw], ps[:, 2 * (i % 2) + c, 0:kw], ACT.Exp,
                                         bias=nmax[:, i % 2, c:c + 1], accum_out=rsum[:, i % 2, c:c + 1]).then_inc(s_exp, 1)

            def weights_hi(h, i):
                act.wait_ge(s_T, h * 4 + i + 1)
                if not at_start(h):
                    act.wait_ge(s_pv, h * 2 + i // 2 - 1)
                nc.scalar.activation(at_hi[i // 2][:, 0:i + 1, (i % 2) * P:(i % 2 + 1) * P],
                                     ps[:, B_AT, 0:(i + 1) * P].rearrange("p (j q) -> p j q", j=i + 1), ACT.Copy).then_inc(s_Thi, 1)

            def v_split(h):
                if not at_start(h):
                    act.wait_ge(s_pv, h * 2)
                nc.scalar.activation(v_hi, v_all[:, :, bass.ds(h * P, P)], ACT.Copy).then_inc(s_vhi, 1)

            def copy_o(h):
                act.wait_ge(s_pv, h * 2 + 2)
                if not at_start(h):
                    act.wait_ge(s_hi, h + 8 * I_O)
                    act.wait_ge(s_lo, h + 8 * I_O)
                    act.wait_ge(s_ost, h)
                nc.scalar.activation(o_sb, ps[:, B_O, :], ACT.Copy).then_inc(s_oc, 1)
                nc.scalar.activation(o_sq, ps[:, B_O, :], ACT.Square).then_inc(s_oc, 1)

            def out_hi(h):
                act.wait_ge(s_on, h + 1)
                nc.scalar.activation(h2[:, 0, bass.ds(h, 1), :].rearrange("p a b -> p (a b)"), o_sb, ACT.Copy).then_inc(s_hi, 1)

            def head(h, b, prev, nxt, more):
                exps(h, 0)
                if prev is not None:
                    weights_hi(prev, 3)
                exps(h, 1)
                if more is not None:
                    n = S_Q + 2 + b if more == "q" else S_WO + (1 if nxt is None else 0)
                    off = h - b if more == "q" else 0
                    act.wait_ge(s_raw[n % RAW], off * 8 + 16 * (n // RAW + 1))
                    act.wait_ge(s_used, off + n - 1)
                    nc.scalar.activation(w_hi[:, n % 2 if more == "q" else slot(n), :], w_raw[:, n % RAW, :],
                                         ACT.Copy).then_inc(s_whi, 1)
                if nxt is not None:
                    copy_q(nxt)
                if prev is not None:
                    copy_o(prev)
                weights_hi(h, 0)
                v_split(h)
                exps(h, 2)
                weights_hi(h, 1)
                exps(h, 3)
                if prev is not None:
                    out_hi(prev)
                if nxt is not None:
                    split_qk(nxt, 1 - b)
                weights_hi(h, 2)

            head(0, 0, None, 1, "q")
            with act.Fori(0, (H - 4) // 2) as it:
                head(it * 2 + 1, 1, it * 2, it * 2 + 2, "q")
                head(it * 2 + 2, 0, it * 2 + 1, it * 2 + 3, "q")
            head(5, 1, 4, 6, "q")
            head(6, 0, 5, 7, "wo")
            head(7, 1, 6, None, "wo")
            weights_hi(H - 1, 3)
            copy_o(H - 1)
            out_hi(H - 1)

            for m in range(KC):
                split(S_WO + m + AHEAD)
                act.wait_ge(s_acc, U_WO + m + 1)
                chunk_hi(I_M1, m, g_m1)
                square(NORM_M1, m)

            def after1(m):
                if m >= 1:
                    copy_out(m - 1)

            def copy_out(m):
                act.wait_ge(s_fT, m + 1)
                nc.scalar.activation(kv[:, m, :], ps[:, BC + m % 2, :], ACT.Copy).then_inc(s_fc, 1)

            mlp(1, S_MLP1, U_MLP1, 3, after1)
            copy_out(KC - 1)

        @block.vector
        def _(dve):
            V = nc.vector
            mixed = [0]

            def mix_step(ins, wait=True):
                mixed[0] += 1
                ins.then_inc(s_mix, 1)
                dve.wait_ge(s_mix, mixed[0])

            def split(n, off=0):
                dve.wait_ge(s_whi, off + n + 1)
                V.tensor_tensor(w_lo[:, slot(n), :], w_raw[:, n % RAW, :], w_hi[:, slot(n), :].bitcast(F32),
                                ALU.subtract).then_inc(s_wlo, 1)

            def chunk_lo(i, m, g):
                dve.wait_ge(s_hi, 8 * i + m + 1)
                V.scalar_tensor_tensor(h_of[i][:, 1, m, :], xT[:, m, :], gains[:, g, m:m + 1],
                                       h_of[i][:, 0, m, :].bitcast(F32), ALU.mult, ALU.subtract).then_inc(s_lo, 1)

            def residual(n, u, m, off=0):
                dve.wait_ge(s_used, off + n + 1)
                V.tensor_tensor(xT[:, m, :], ps[:, u % ACC, :], xT[:, m, :], ALU.add).then_inc(s_acc, 1)

            def mean_squares(i):
                dve.wait_ge(s_nst, i + 1)
                V.tensor_scalar(nms[:, i, :], ps[:, STAT, 0:2 * TB].rearrange("p (t c) -> p t c", c=2)[:, :, 0], 1.0 / D, EPS,
                                ALU.mult, ALU.add).then_inc(s_nms, 1)

            V.memset(ones2[:], 1.0).then_inc(s_cst, 1)
            V.memset(comp2[:], 0.0).then_inc(s_cst, 1)
            dve.wait_ge(s_cst, 2)
            V.memset(comp2[0:HD, 0:1], 1.0).then_inc(s_cst, 1)
            V.memset(comp2[HD:P, 1:2], 1.0).then_inc(s_cst, 1)
            V.memset(mix[2][:, 0:2], 0.0).then_inc(s_mix, 1)
            mixed[0] += 1
            dve.wait_ge(s_zero, 3)
            V.tensor_copy(identb[:], ident[:]).then_inc(s_cst, 1)
            for t in range(TB):
                dve.wait_ge(s_xt, 2 * t + 1)
                V.tensor_copy(xT[:, 0:4, t * P:(t + 1) * P],
                              ps[:, 2 * t, :].rearrange("p (k q) -> p k q", k=4)).then_inc(s_xd, 1)
            dve.wait_ge(s_par, 16 * 14)
            dve.wait_ge(s_xd, TB)
            dve.wait_ge(s_xa, TB)
            split(0)
            for m in range(KC):
                chunk_lo(I_A, m, g_a)
                if m == 3:
                    split(1)
            for i in range(2):
                V.tensor_tensor_reduce(out=lamp[:], in0=lamv[:, 2 * i, :], in1=lamv[:, 2 * i + 1, :], scale=1.0, scalar=0.0,
                                       op0=ALU.mult, op1=ALU.add, accum_out=lams[:, i:i + 1]).then_inc(s_cst, 1)
                dve.wait_ge(s_cst, 6 + i)
            for i, c in enumerate((HD ** -0.5, 1.0, 1.0 - LAM_INIT)):
                V.tensor_scalar(hgs[:, i:i + 1], hg[:, i:i + 1], c, None, ALU.mult).then_inc(s_cst, 1)
            dve.wait_ge(s_lam, 1)
            V.tensor_tensor(lams[:, 4:5], lams[:, 3:4], lams[:, 2:3], ALU.subtract).then_inc(s_cst, 1)
            dve.wait_ge(s_cst, 11)
            V.tensor_scalar(lams[:, 5:6], lams[:, 4:5], -LAM_INIT, None, ALU.add).then_inc(s_cst, 1)
            mean_squares(NORM_A)

            cr, u, t0, br = mix[0], work[:, U0:U0 + T + 2], mix[1], mix[4]
            for n in range(N_IN):
                split(n + AHEAD)
                if n == 0:
                    dve.wait_ge(s_rB, 1)
                j = n // 3
                acc = ps[:, (U_IN + n) % ACC, :]
                dve.wait_ge(s_used, n + 1)
                if n % 3 == 0:
                    V.tensor_tensor(cr, acc, rB[:], ALU.mult).then_inc(s_acc, 1)
                    dve.wait_ge(s_acc, n + 1)
                    mix_step(V.tensor_tensor(cr, cr, rB[:], ALU.mult))
                elif n % 3 == 1:
                    V.tensor_tensor(u[:, 2:T + 2], acc, cr, ALU.mult).then_inc(s_acc, 1)
                    dve.wait_ge(s_acc, n + 1)
                    mix_step(V.tensor_scalar(t0, u[:, 0:T], conv[:, 0, j:j + 1], None, ALU.mult))
                    mix_step(V.scalar_tensor_tensor(t0, u[:, 1:T + 1], conv[:, 1, j:j + 1], t0, ALU.mult, ALU.add))
                    mix_step(V.scalar_tensor_tensor(t0, u[:, 2:T + 2], conv[:, 2, j:j + 1], t0, ALU.mult, ALU.add))
                else:
                    V.tensor_tensor(br, acc, rB[:], ALU.mult).then_inc(s_acc, 1)
                    dve.wait_ge(s_acc, n + 1)
                    if j >= 2:
                        dve.wait_ge(s_hi, 8 * I_Z + j - 1)
                    z = mix[5 + j % 2]
                    V.tensor_tensor(z, br, t0, ALU.mult).then_inc(s_mix, 9 * (j + 1) - mixed[0])
                    mixed[0] = 9 * (j + 1)
                    dve.wait_ge(s_mix, mixed[0])
                    dve.wait_ge(s_hi, 8 * I_Z + j + 1)
                    V.tensor_tensor(h2[:, 1, j, :], z, h2[:, 0, j, :].bitcast(F32), ALU.subtract).then_inc(s_lo, 1)
            for m in range(KC):
                split(S_OUT + m + AHEAD)
                residual(S_OUT + m, U_OUT + m, m)
                dve.wait_ge(s_acc, U_OUT + m + 1)
                chunk_lo(I_M0, m, g_m0)

            def mlp(layer, base, ubase, norm, scales, after):
                def unit(j, q):
                    c = 32 * layer + j + 1
                    dve.wait_ge(s_used, q * 16 + base + j + 1)
                    if not (at_start(q) and layer == 0 and j < 2):
                        dve.wait_ge(s_ahi, q * 8 + c - 2)
                    V.scalar_tensor_tensor(mix[j % 2], ps[:, (ubase + j) % ACC, :], 0.0, rB[:], ALU.max, ALU.mult).then_inc(s_r, 1)
                    dve.wait_ge(s_r, q * 8 + c)
                    V.tensor_tensor(mix[2], mix[j % 2], mix[j % 2], ALU.mult).then_inc(s_acc, 1)
                    dve.wait_ge(s_acc, q * 16 + ubase + j + 1)
                    dve.wait_ge(s_ahi, q * 8 + c)
                    V.tensor_tensor(ah[:, 8 + j, :], mix[2], ah[:, j, :].bitcast(F32), ALU.subtract).then_inc(s_alo, 1)

                def quarter(q, first=False, last=False):
                    for j in range(8):
                        split(base + j + AHEAD, q * 16)
                        if first and j == 0:
                            mean_squares(norm)
                        if first and j == 1:
                            dve.wait_ge(s_rB, scales)
                        for jj in ((0, 1) if j == 1 else () if j == 0 else (j,)):
                            unit(jj, q)
                    for m in range(8):
                        n = base + 8 + m
                        if not (last and n + AHEAD + q * 16 >= S_END):
                            split(n + AHEAD, q * 16)
                        residual(n, ubase + 8 + m, m, q * 16)
                        if last:
                            after(m)

                quarter(0, first=True)
                with dve.Fori(1, NQ - 1) as q:
                    quarter(q)
                quarter(NQ - 1, last=True)

            def after0(m):
                dve.wait_ge(s_acc, U_MLP0 + 56 + m + 1)
                chunk_lo(I_KV, m, g_kv)

            mlp(0, S_MLP0, U_MLP0, NORM_M0, 2, after0)

            for n in range(8):
                split(S_V + n + AHEAD)
                if n == 0:
                    mean_squares(NORM_B)
                chunk_lo(I_Q, n, g_b)
                if n % 4 == 3:
                    g = n // 4
                    dve.wait_ge(s_nrc, NORM_B + 1)
                    dve.wait_ge(s_used, S_V + n + 1)
                    for t in range(TB):
                        V.tensor_scalar(v_all[:, t, g * T:(g + 1) * T], ps[:, (U_V + t) % ACC, :], rcol[:, NORM_B, t:t + 1], None,
                                        ALU.mult).then_inc(s_acc, 1)
            V.scalar_tensor_tensor(r2[:], rcol[:, NORM_B, :], 1.0 / HD, rcol[:, NORM_B, :], ALU.mult, ALU.mult).then_inc(s_cst, 1)
            dve.wait_ge(s_cst, 13)

            def head_ms(i, b, bank, at):
                dve.wait_ge(s_qst, i + 1)
                if not (isinstance(i, int) and i < 2):
                    dve.wait_ge(s_qrs, i * 2 - 3)
                V.tensor_tensor(qms[:, b, :].rearrange("p (t c) -> p t c", c=2),
                                ps[:, bank, at:at + 8].rearrange("p (t c) -> p t c", c=2),
                                r2[:].unsqueeze(2).to_broadcast([P, TB, 2]), ALU.mult).then_inc(s_qms, 1)
                dve.wait_ge(s_qms, i * 2 + 1)
                V.tensor_scalar(qms[:, b, :], qms[:, b, :], EPS, None, ALU.add).then_inc(s_qms, 1)

            def k_norm_step(h):
                dve.wait_ge(s_qbc, h + 1)
                V.scalar_tensor_tensor(kv[:, h, :], raw_qk[h % 2], hgs[:, 1:2], ps[:, BC, :], ALU.mult, ALU.mult).then_inc(s_qn, 1)

            for h in range(H):
                split(S_K + h + AHEAD)
                if h >= 1:
                    head_ms(h - 1, (h - 1) % 2, STAT, 0)
                dve.wait_ge(s_used, S_K + h + 1)
                V.tensor_copy(raw_qk[h % 2], ps[:, (U_K + h) % ACC, :]).then_inc(s_acc, 1)
                dve.wait_ge(s_acc, U_K + h + 1)
                V.memset(lamp[:, 0:1], 0.0).then_inc(s_qc, 1)
                if h >= 1:
                    k_norm_step(h - 1)
            head_ms(H - 1, 1, STAT, 0)
            k_norm_step(H - 1)
            dve.wait_ge(s_used, S_V)

            def normalise_q(i):
                dve.wait_ge(s_qbc, i + 1)
                V.scalar_tensor_tensor(raw_qk[0], raw_qk[0], hgs[:, 0:1], ps[:, B_BC, :], ALU.mult, ALU.mult).then_inc(s_qn, 1)

            def split_qk(h, b):
                dve.wait_ge(s_qhi, h * 2 + 1)
                V.tensor_tensor(q_lo[b], raw_qk[0], q_hi[b].bitcast(F32), ALU.subtract).then_inc(s_qlo, 1)
                dve.wait_ge(s_qhi, h * 2 + 2)
                V.tensor_tensor(k_lo[b], kv[:, bass.ds(h, 1), :].rearrange("p a b -> p (a b)"), k_hi[b].bitcast(F32),
                                ALU.subtract).then_inc(s_qlo, 1)

            head_ms(H, 0, B_Q, 8)
            normalise_q(H)
            split_qk(0, 0)

            def softmax(h, i):
                b = i % 2
                kw = (i + 1) * P
                p1, p2 = p_buf[b][:, 0, 0:kw], p_buf[b][:, 1, 0:kw]
                dve.wait_ge(s_S, h * 4 + i + 1)
                if not (at_start(h) and i < 2):
                    dve.wait_ge(s_exp, h * 8 + 2 * i - 2)
                V.tensor_reduce(nmax[:, b, :], ps[:, 2 * b:2 * b + 2, 0:kw], AX_X, ALU.max, negate=True).then_inc(s_mx, 1)
                dve.wait_ge(s_exp, h * 8 + 2 * i + 2)
                V.reciprocal(rinv[:, b, :], rsum[:, b, :]).then_inc(s_sc, 1)
                dve.wait_ge(s_sc, h * 12 + 3 * i + 1)
                V.tensor_tensor(lrin[:, b:b + 1], rinv[:, b, 1:2], lams[:, 5:6], ALU.mult).then_inc(s_sc, 1)
                dve.wait_ge(s_sc, h * 12 + 3 * i + 2)
                V.tensor_scalar(p2, p2, lrin[:, b:b + 1], None, ALU.mult).then_inc(s_sc, 1)
                dve.wait_ge(s_sc, h * 12 + 3 * i + 3)
                V.scalar_tensor_tensor(p1, p1, rinv[:, b, 0:1], p2, ALU.mult, ALU.add).then_inc(s_at, 1)

            def weights_lo(h, i):
                dve.wait_ge(s_Thi, h * 4 + i + 1)
                cols = slice((i % 2) * P, (i % 2 + 1) * P)
                V.tensor_tensor(at_lo[i // 2][:, 0:i + 1, cols], ps[:, B_AT, 0:(i + 1) * P].rearrange("p (j q) -> p j q", j=i + 1),
                                at_hi[i // 2][:, 0:i + 1, cols].bitcast(F32), ALU.subtract).then_inc(s_Tlo, 1)

            def v_split(h):
                dve.wait_ge(s_vhi, h + 1)
                V.tensor_tensor(v_lo, v_all[:, :, bass.ds(h * P, P)], v_hi.bitcast(F32), ALU.subtract).then_inc(s_vlo, 1)

            def out_ms(h):
                dve.wait_ge(s_ost, h + 1)
                if not at_start(h):
                    dve.wait_ge(s_ors, h)
                V.tensor_scalar(oms[:], ps[:, B_Q, 0:8], 1.0 / P, EPS, ALU.mult, ALU.add).then_inc(s_oms, 1)

            def out_norm(h):
                dve.wait_ge(s_obc, h + 1)
                V.scalar_tensor_tensor(o_sb, o_sb, hgs[:, 2:3], ps[:, B_BC, :], ALU.mult, ALU.mult).then_inc(s_on, 1)

            def out_lo(h):
                dve.wait_ge(s_hi, h + (8 * I_O + 1))
                V.tensor_tensor(h2[:, 1, bass.ds(h, 1), :].rearrange("p a b -> p (a b)"), o_sb,
                                h2[:, 0, bass.ds(h, 1), :].rearrange("p a b -> p (a b)").bitcast(F32),
                                ALU.subtract).then_inc(s_lo, 1)

            def head(h, b, prev, nxt, more):
                softmax(h, 0)
                if prev is not None:
                    weights_lo(prev, 3)
                softmax(h, 1)
                if more is not None:
                    n = S_Q + 2 + b if more == "q" else S_WO + (1 if nxt is None else 0)
                    off = h - b if more == "q" else 0
                    sl = n % 2 if more == "q" else slot(n)
                    dve.wait_ge(s_whi, off + n + 1)
                    V.tensor_tensor(w_lo[:, sl, :], w_raw[:, n % RAW, :], w_hi[:, sl, :].bitcast(F32),
                                    ALU.subtract).then_inc(s_wlo, 1)
                weights_lo(h, 0)
                v_split(h)
                softmax(h, 2)
                if prev is not None:
                    out_ms(prev)
                if nxt is not None:
                    head_ms(nxt + H, 1 - b, B_Q, 8)
                weights_lo(h, 1)
                softmax(h, 3)
                if prev is not None:
                    out_norm(prev)
                    out_lo(prev)
                if nxt is not None:
                    normalise_q(nxt + H)
                    split_qk(nxt, 1 - b)
                weights_lo(h, 2)

            head(0, 0, None, 1, "q")
            with dve.Fori(0, (H - 4) // 2) as it:
                head(it * 2 + 1, 1, it * 2, it * 2 + 2, "q")
                head(it * 2 + 2, 0, it * 2 + 1, it * 2 + 3, "q")
            head(5, 1, 4, 6, "q")
            head(6, 0, 5, 7, "wo")
            head(7, 1, 6, None, "wo")
            weights_lo(H - 1, 3)
            out_ms(H - 1)
            out_norm(H - 1)
            out_lo(H - 1)

            for m in range(KC):
                split(S_WO + m + AHEAD)
                residual(S_WO + m, U_WO + m, m)
                dve.wait_ge(s_acc, U_WO + m + 1)
                chunk_lo(I_M1, m, g_m1)
            mlp(1, S_MLP1, U_MLP1, NORM_M1, 3, lambda m: None)


_INS = ["x", "a_norm", "a_w_in", "a_conv", "a_w_out", "kv_norm", "w_kv", "k_norm", "b_norm", "w_q", "q_norm",
        "lam_q1", "lam_k1", "lam_q2", "lam_k2", "sub_norm", "w_o", "mlp_norm", "w_up", "w_down"]


def kernel(**inputs):
    import numpy as np
    import concourse.bacc as bacc
    from concourse.bass_utils import run_bass_kernel_spmd

    nc = bacc.Bacc("TRN2", target_bir_lowering=False, num_devices=1)
    arrays, args = {}, []
    for name in _INS:
        a = np.ascontiguousarray(inputs[name])
        arrays[f"in_{name}"] = a
        args.append(nc.dram_tensor(f"in_{name}", a.shape, mybir.dt.from_np(a.dtype), kind="ExternalInput").ap())
    out = nc.dram_tensor("out_x", (1, T, D), F32, kind="ExternalOutput").ap()
    build(nc, *args, out)
    r = run_bass_kernel_spmd(nc, [arrays], core_ids=[0])
    return r.results[0]["out_x"]
```

```python
import math
from contextlib import ExitStack

import concourse.bass as bass
from concourse import mybir


F32 = mybir.dt.float32
F32R = mybir.dt.float32r
BF16 = mybir.dt.bfloat16
ALU = mybir.AluOpType
ACT = mybir.ActivationFunctionType
AX_X = mybir.AxisListType.X

P = 128
T = 512
TB = T // P
D = 1024
KC = D // P
F = 4 * D
NQ = 4
H = 8
HD = 64
EPS = 1e-6
NEG = -1e30
LAM_INIT = 0.8 - 0.6 * math.exp(-0.3 * 1)
SLAB = 1024

RAW = 2
RING = 4
AHEAD = 2
ACC = 4
BC, STAT = 6, 7
B_Q, B_AT, B_O, B_BC = 4, 5, 6, 7
HEAD_AHEAD = 2

N_IN, N_OUT = 24, 8
S_IN = 0
S_OUT = S_IN + N_IN
S_MLP0 = S_OUT + N_OUT
S_V = S_MLP0 + NQ * 16
S_K = S_V + 8
S_Q = S_K + 8
S_WO = S_Q + H
S_MLP1 = S_WO + 8
S_END = S_MLP1 + NQ * 16

U_IN, U_OUT, U_MLP0, U_V, U_K, U_WO, U_MLP1 = 0, 24, 32, 96, 104, 114, 122

I_A, I_Z, I_M0, I_KV, I_Q, I_O, I_M1 = range(7)
NORM_A, NORM_M0, NORM_B, NORM_M1 = range(4)


def slot(n):
    return (n % 2) if S_Q <= n < S_WO else n % RING


def freed(n):
    if n >= S_WO and n < S_WO + 2:
        return n - 1
    if S_Q + 2 <= n < S_WO:
        return n - 1
    return n - RING + 1 if n >= RING else 0


def at_start(i):
    return isinstance(i, int) and i == 0


def heads(engine, head):
    head(0, 0, None, 1, 2)
    head(1, 1, 0, 2, 3)
    with engine.Fori(0, (H - 4) // 2) as it:
        head(it * 2 + 2, 0, it * 2 + 1, it * 2 + 3, it * 2 + 4)
        head(it * 2 + 3, 1, it * 2 + 2, it * 2 + 4, it * 2 + 5)
    head(H - 2, 0, H - 3, H - 1, None)
    head(H - 1, 1, H - 2, None, None)


def build(nc, x, a_norm, a_w_in, a_conv, a_w_out, kv_norm, w_kv, k_norm, b_norm, w_q, q_norm,
          lam_q1, lam_k1, lam_q2, lam_k2, sub_norm, w_o, mlp_norm, w_up, w_down, out):
    with ExitStack() as ctx:
        def sb(name, shape, dt=F32):
            return ctx.enter_context(nc.sbuf_tensor(name, shape, dt))

        def sem(name):
            return ctx.enter_context(nc.semaphore(name))

        xT = sb("xT", [P, KC, T])
        h1 = sb("h1", [P, 2, KC, T], F32R)
        h2 = sb("h2", [P, 2, KC, T], F32R)
        ah = sb("ah", [P, 16, T], F32R)
        kv = sb("kv", [P, 16, T])
        w_raw = sb("w_raw", [P, RAW, SLAB])
        w_hi = sb("w_hi", [P, RING, SLAB], F32R)
        w_lo = sb("w_lo", [P, RING, SLAB], F32R)
        rB = sb("rB", [P, T])
        work = sb("work", [P, 4096])
        sqsum = work[:, 3584:4096]
        ident = sb("ident", [P, P])
        identb = sb("identb", [P, P], BF16)
        maskb = sb("maskb", [P, P], BF16)
        comp2 = sb("comp2", [P, 2])
        ones2 = sb("ones2", [P, 2])
        mhalf = sb("mhalf", [P, 8])
        gains = sb("gains", [P, 5, KC])
        conv = sb("conv", [P, 3, KC])
        hg = sb("hg", [P, 3])
        hgs = sb("hgs", [P, 3])
        lamv = sb("lamv", [P, 4, HD])
        lamp = sb("lamp", [P, HD])
        lams = sb("lams", [P, 8])
        nms = sb("nms", [P, 4, TB])
        rcol = sb("rcol", [P, 4, TB])
        r2 = sb("r2", [P, TB])
        qms = sb("qms", [P, 2, 8])
        qpw = sb("qpw", [P, 8])
        oms = sb("oms", [P, 8])
        ors = sb("ors", [P, 8])
        nmax = sb("nmax", [P, 2, 2])
        rsum = sb("rsum", [P, 2, 2])
        rinv = sb("rinv", [P, 2, 2])
        ps = ctx.enter_context(nc.psum_tensor("ps", [P, 8, T], F32))

        g_a, g_m0, g_m1, g_kv, g_b = range(5)
        mix = [work[:, i * T:(i + 1) * T] for i in range(7)]
        U0 = 2 * T
        sqb = [work[:, 6 * T - 1024 + i * T:6 * T - 1024 + (i + 1) * T] for i in range(2)]
        p_buf = [work[:, (4 + 2 * i) * T:(6 + 2 * i) * T].rearrange("p (c k) -> p c k", c=2) for i in range(2)]
        at_hi = [ah[:, 0, :].rearrange("p (j q) -> p j q", j=2), ah[:, 2:4, :].rearrange("p a (j q) -> p (a j) q", j=2)]
        at_lo = [ah[:, 1, :].rearrange("p (j q) -> p j q", j=2), ah[:, 4:6, :].rearrange("p a (j q) -> p (a j) q", j=2)]
        q_hi, q_lo = [ah[:, 6 + 2 * b, :] for b in range(2)], [ah[:, 7 + 2 * b, :] for b in range(2)]
        k_hi, k_lo = [ah[:, 10 + 2 * b, :] for b in range(2)], [ah[:, 11 + 2 * b, :] for b in range(2)]
        v_hi, v_lo = ah[:, 14, :].rearrange("p (t e) -> p t e", t=TB), ah[:, 15, :].rearrange("p (t e) -> p t e", t=TB)
        v_all = kv[:, 8:16, :].rearrange("p a b -> p (a b)").rearrange("p (t f) -> p t f", t=TB)
        x_tok = kv[:, 0:8, :].rearrange("p a b -> p (a b)").rearrange("p (t f) -> p t f", t=TB)
        raw_qk = [work[:, 0:T], work[:, 2 * T:3 * T]]
        sq_qk = [work[:, T:2 * T], work[:, 3 * T:4 * T]]
        o_sb, o_sq = work[:, 2 * T:3 * T], work[:, 3 * T:4 * T]
        h_of = [h1, h2, h1, h2, h1, h2, h1]

        s_x = [sem(f"s_x{t}") for t in range(TB)]
        s_par = sem("s_par")
        s_raw = [sem(f"s_raw{i}") for i in range(RAW)]
        s_whi = sem("s_whi")
        s_wlo = sem("s_wlo")
        s_used = sem("s_used")
        s_acc = sem("s_acc")
        s_zero = sem("s_zero")
        s_cst = sem("s_cst")
        s_xt = sem("s_xt")
        s_xd = sem("s_xd")
        s_xa = sem("s_xa")
        s_hi = sem("s_hi")
        s_lo = sem("s_lo")
        s_sq = sem("s_sq")
        s_add = sem("s_add")
        s_nst = sem("s_nst")
        s_nms = sem("s_nms")
        s_nrc = sem("s_nrc")
        s_nbc = sem("s_nbc")
        s_rB = sem("s_rB")
        s_mix = sem("s_mix")
        s_r = sem("s_r")
        s_ahi = sem("s_ahi")
        s_alo = sem("s_alo")
        s_lam = sem("s_lam")
        s_qc = sem("s_qc")
        s_qsq = sem("s_qsq")
        s_qst = sem("s_qst")
        s_qms = sem("s_qms")
        s_qrs = sem("s_qrs")
        s_qbc = sem("s_qbc")
        s_qn = sem("s_qn")
        s_qhi = sem("s_qhi")
        s_qlo = sem("s_qlo")
        s_vhi = sem("s_vhi")
        s_vlo = sem("s_vlo")
        s_S = sem("s_S")
        s_mx = sem("s_mx")
        s_exp = sem("s_exp")
        s_sc = sem("s_sc")
        s_at = sem("s_at")
        s_T = sem("s_T")
        s_Thi = sem("s_Thi")
        s_Tlo = sem("s_Tlo")
        s_pv = sem("s_pv")
        s_oc = sem("s_oc")
        s_ost = sem("s_ost")
        s_oms = sem("s_oms")
        s_ors = sem("s_ors")
        s_obc = sem("s_obc")
        s_on = sem("s_on")
        s_fT = sem("s_fT")
        s_fc = sem("s_fc")
        s_out = sem("s_out")

        win_d = a_w_in.rearrange("l (k p) c -> p (l k) c", p=P)
        wout_d = a_w_out.rearrange("l (k p) c -> p (l k) c", p=P)
        wkv_d = w_kv.rearrange("(k p) c -> p k c", p=P)
        wq_d = w_q.rearrange("l (k p) c -> p (l k) c", p=P)
        wo_d = w_o.rearrange("l (k p) c -> p (l k) c", p=P)
        up_d = [w_up[l].rearrange("(k p) c -> p k c", p=P) for l in range(2)]
        dn_d = [w_down[l].rearrange("(k p) c -> p k c", p=P) for l in range(2)]
        out_d = out.rearrange("b (t p) d -> p (b t) d", p=P)
        x_d = x.rearrange("b (t p) d -> p (b t) d", p=P)

        block = ctx.enter_context(nc.Block())

        @block.sync
        def _(sp):
            def load(n, src, off=0):
                if n >= RAW:
                    sp.wait_ge(s_wlo, off + n - RAW + 1)
                dst = w_raw[:, n % RAW, :].rearrange("p (k c) -> p k c", k=src.shape[1])
                sp.dma_start(dst, src).then_inc(s_raw[n % RAW], 16)

            for t in range(TB):
                sp.dma_start(x_tok[:, t, :], x_d[:, t, :]).then_inc(s_x[t], 16)

            def cols(w, c):
                return w[:, :, c * P:(c + 1) * P]

            for j in range(KC):
                for i, part in enumerate((1, 2, 0)):
                    load(S_IN + 3 * j + i, cols(win_d, part * KC + j))
            for m in range(KC):
                load(S_OUT + m, cols(wout_d, m))

            def mlp(layer, base):
                with sp.Fori(0, NQ) as q:
                    for j in range(8):
                        load(base + j, up_d[layer][:, :, bass.ds(q * D + j * P, P)], q * 16)
                    for m in range(8):
                        load(base + 8 + m, dn_d[layer][:, bass.ds(q * KC, KC), m * P:(m + 1) * P], q * 16)

            mlp(0, S_MLP0)
            for n in range(8):
                g, kk = n // 4, n % 4
                load(S_V + n, wkv_d[:, 2 * kk:2 * kk + 2, D + g * T:D + (g + 1) * T])
            for h in range(H):
                load(S_K + h, cols(wkv_d, h))
            for h in range(H):
                load(S_Q + h, cols(wq_d, h))
            for m in range(KC):
                load(S_WO + m, cols(wo_d, m))
            mlp(1, S_MLP1)
            for m in range(KC):
                sp.wait_ge(s_fc, m + 1)
                sp.dma_start(out_d[:, :, m * P:(m + 1) * P],
                             kv[:, m, :].rearrange("p (t c) -> p t c", t=TB)).then_inc(s_out, 16)
            sp.wait_ge(s_out, 16 * KC)

        @block.gpsimd
        def _(pool):
            nc.gpsimd.memset(ident[:], 0.0).then_inc(s_zero, 1)
            nc.gpsimd.memset(maskb[:], 0.0).then_inc(s_zero, 1)
            pool.wait_ge(s_zero, 2)
            nc.gpsimd.affine_select(out=ident[:], in_=ident[:], compare_op=ALU.not_equal, fill=1.0, base=0,
                                    pattern=[[-1, P]], channel_multiplier=1).then_inc(s_zero, 1)
            nc.gpsimd.affine_select(out=maskb[:], in_=maskb[:], compare_op=ALU.is_ge, fill=NEG, base=0,
                                    pattern=[[-1, P]], channel_multiplier=1).then_inc(s_zero, 1)
            nc.gpsimd.memset(mhalf[:], -0.5).then_inc(s_zero, 1)
            zero = [(t, b, j) for t in (at_hi, at_lo) for b, j in ((0, 1), (1, 3))]

            def norm(i):
                if i > 0:
                    pool.wait_ge(s_nst, i)
                nc.gpsimd.memset(sqsum, 0.0).then_inc(s_zero, 1)
                pool.wait_ge(s_zero, 6 + i + (4 if i == NORM_M1 else 0))
                for m in range(KC):
                    pool.wait_ge(s_sq, 8 * i + m + 1)
                    nc.gpsimd.tensor_tensor(sqsum, sqsum, sqb[m % 2], ALU.add).then_inc(s_add, 1)
                    pool.wait_ge(s_add, 8 * i + m + 1)
                pool.wait_ge(s_nms, i + 1)
                nc.gpsimd.tensor_tensor(rcol[:, i, :], nms[:, i, :], mhalf[:, 0:TB], ALU.pow).then_inc(s_nrc, 1)

            norm(NORM_A)
            norm(NORM_M0)
            norm(NORM_B)

            def head_scale(i, b, sq):
                pool.wait_ge(s_qms, i * 2 + 2)
                nc.gpsimd.tensor_tensor(qpw[:], qms[:, b, :], mhalf[:], ALU.pow).then_inc(s_qrs, 1)
                pool.wait_ge(s_qrs, i * 2 + 1)
                nc.gpsimd.tensor_tensor(sq.rearrange("p (t c d) -> p t c d", t=TB, c=2),
                                        qpw[:].rearrange("p (t c) -> p t c", c=2).unsqueeze(3).to_broadcast([P, TB, 2, HD]),
                                        rcol[:, NORM_B, :].unsqueeze(2).unsqueeze(3).to_broadcast([P, TB, 2, HD]),
                                        ALU.mult).then_inc(s_qrs, 1)

            def out_scale(h):
                pool.wait_ge(s_oms, h + 1)
                nc.gpsimd.tensor_tensor(ors[:], oms[:], mhalf[:], ALU.pow).then_inc(s_ors, 1)

            pool.wait_ge(s_alo, 32)
            pool.wait_ge(s_used, S_V)
            for t, b, j in zero:
                nc.gpsimd.memset(t[b][:, j, 0:P].bitcast(F32), 0.0).then_inc(s_zero, 1)
            for i in range(H + 2):
                head_scale(i, i % 2, sq_qk[i % 2])

            def k_lo_part(h, b):
                pool.wait_ge(s_qhi, h * 2 + 1)
                nc.gpsimd.tensor_tensor(k_lo[b], kv[:, bass.ds(h, 1), :].rearrange("p a b -> p (a b)"), k_hi[b].bitcast(F32),
                                        ALU.subtract).then_inc(s_qlo, 1)

            def q_lo_part(h, b, raw):
                pool.wait_ge(s_qhi, h * 2 + 2)
                nc.gpsimd.tensor_tensor(q_lo[b], raw, q_hi[b].bitcast(F32), ALU.subtract).then_inc(s_qlo, 1)

            def v_split(h):
                pool.wait_ge(s_vhi, h + 1)
                nc.gpsimd.tensor_tensor(v_lo, v_all[:, :, bass.ds(h * P, P)], v_hi.bitcast(F32), ALU.subtract).then_inc(s_vlo, 1)

            def out_lo(h):
                pool.wait_ge(s_hi, h + (8 * I_O + 1))
                nc.gpsimd.tensor_tensor(h2[:, 1, bass.ds(h, 1), :].rearrange("p a b -> p (a b)"), o_sb,
                                        h2[:, 0, bass.ds(h, 1), :].rearrange("p a b -> p (a b)").bitcast(F32),
                                        ALU.subtract).then_inc(s_lo, 1)

            def head(h, b, prev, nxt, far):
                new_q = prev is not None and nxt is not None
                if new_q:
                    k_lo_part(nxt, 1 - b)
                    q_lo_part(nxt, 1 - b, raw_qk[0])
                v_split(h)
                if prev is not None:
                    out_scale(prev)
                if far is not None:
                    head_scale(far + H, b, sq_qk[0])
                if prev is not None:
                    out_lo(prev)

            for h in range(2):
                k_lo_part(h, h)
                q_lo_part(h, h, raw_qk[h])
            heads(pool, head)
            out_scale(H - 1)
            out_lo(H - 1)
            norm(NORM_M1)

        @block.tensor
        def _(pe):
            def wait_slab(n, off=0):
                pe.wait_ge(s_wlo, off + n + 1)

            def wait_acc(u, off=0):
                if u >= ACC:
                    pe.wait_ge(s_acc, off + u - ACC + 1)

            def product(bank, n, src, ks, wait_chunk=None, ks0=0, total=KC):
                s = slot(n)
                for k in ks:
                    if wait_chunk is not None:
                        wait_chunk(k)
                    for i, (w, half) in enumerate(((w_hi, 0), (w_hi, 1), (w_lo, 0))):
                        last = nc.tensor.matmul(ps[:, bank, :], w[:, s, k * P:(k + 1) * P], src(half, k),
                                                start=(k == 0 and i == 0), stop=(k == total - 1 and i == 2))
                return last

            def operand(i):
                return lambda half, k: h_of[i][:, half, k, :]

            def chunks_of(i):
                return lambda k: pe.wait_ge(s_lo, 8 * i + k + 1)

            def dense(n, u, i, first=False):
                wait_acc(u)
                wait_slab(n)
                product(u % ACC, n, operand(i), range(KC), chunks_of(i) if first else None).then_inc(s_used, 1)

            def norm_sums(i):
                pe.wait_ge(s_add, 8 * (i + 1))
                for t in range(TB):
                    last = nc.tensor.matmul(ps[:, STAT, 2 * t:2 * t + 2], sqsum[:, t * P:(t + 1) * P], ones2[:],
                                            start=True, stop=True)
                last.then_inc(s_nst, 1)

            def spread(bank, col, done, times=P):
                for t in range(TB):
                    last = nc.tensor.matmul(ps[:, bank, t * P:(t + 1) * P], col(t), ident[:], start=True, stop=True)
                last.then_inc(done, 1)

            def norm_spread(i):
                pe.wait_ge(s_nrc, i + 1)
                spread(BC, lambda t: rcol[:, i, t:t + 1].to_broadcast([P, P]), s_nbc)

            pe.wait_ge(s_zero, 5)
            pe.wait_ge(s_cst, 5)
            for t in range(TB):
                pe.wait_ge(s_x[t], 16)
                for hf in range(2):
                    for k in range(4):
                        c = (4 * hf + k) * P
                        last = nc.tensor.transpose(ps[:, 2 * t + hf, k * P:(k + 1) * P], x_tok[:, t, c:c + P], ident[:])
                    last.then_inc(s_xt, 1)
            pe.wait_ge(s_xd, TB)
            pe.wait_ge(s_xa, TB)

            for n in range(N_IN):
                dense(S_IN + n, U_IN + n, I_A, n == 0)
                if n == 0:
                    norm_sums(NORM_A)
                if n == 1:
                    norm_spread(NORM_A)
            for m in range(KC):
                dense(S_OUT + m, U_OUT + m, I_Z, m == 0)

            def mlp(layer, base, ubase, inp, norm):
                def quarter(q, first=False, last=False):
                    for j in range(8):
                        wait_acc(ubase + j, q * 16)
                        wait_slab(base + j, q * 16)
                        product((ubase + j) % ACC, base + j, operand(inp), range(KC),
                                chunks_of(inp) if first and j == 0 else None).then_inc(s_used, 1)
                        if first and j == 0:
                            norm_sums(norm)
                        if first and j == 1:
                            norm_spread(norm)
                    for m in range(8):
                        wait_acc(ubase + 8 + m, q * 16)
                        wait_slab(base + 8 + m, q * 16)

                        def act_chunk(k):
                            pe.wait_ge(s_alo, q * 8 + (32 * layer + k + 1))
                        product((ubase + m) % ACC, base + 8 + m, lambda half, k: ah[:, 8 * half + k, :],
                                range(KC), act_chunk if m == 0 else None).then_inc(s_used, 1)
                        if last and layer == 1 and m >= 1:
                            final(m - 1)
                    if last and layer == 1:
                        final(KC - 1)

                quarter(0, first=True)
                with pe.Fori(1, NQ - 1) as q:
                    quarter(q)
                quarter(NQ - 1, last=True)

            def final(m):
                pe.wait_ge(s_acc, U_MLP1 + 16 * (NQ - 1) + 8 + m + 1)
                if m >= 2:
                    pe.wait_ge(s_fc, m - 1)
                for t in range(TB):
                    last = nc.tensor.transpose(ps[:, BC + m % 2, t * P:(t + 1) * P], xT[:, m, t * P:(t + 1) * P], ident[:])
                last.then_inc(s_fT, 1)

            mlp(0, S_MLP0, U_MLP0, I_M0, NORM_M0)

            for g in range(2):
                for kk in range(4):
                    n = S_V + 4 * g + kk
                    wait_slab(n)
                    s = slot(n)
                    for t in range(TB):
                        if kk == 0:
                            wait_acc(U_V + 4 * g + t)
                        for k2 in range(2):
                            k = 2 * kk + k2
                            if g == 0 and t == 0:
                                pe.wait_ge(s_lo, 8 * I_KV + k + 1)
                            for i, (half, w) in enumerate(((0, w_hi), (0, w_lo), (1, w_hi))):
                                last = nc.tensor.matmul(ps[:, (U_V + t) % ACC, :], h2[:, half, k, t * P:(t + 1) * P],
                                                        w[:, s, k2 * T:(k2 + 1) * T],
                                                        start=(k == 0 and i == 0), stop=(k == KC - 1 and i == 2))
                    last.then_inc(s_used, 1)
                    if g == 0 and kk == 0:
                        norm_sums(NORM_B)

            def head_sums(i, sq, bank, at):
                pe.wait_ge(s_qsq, i + 1)
                if not at_start(i):
                    pe.wait_ge(s_qms, i * 2)
                for t in range(TB):
                    last = nc.tensor.matmul(ps[:, bank, at + 2 * t:at + 2 * t + 2], sq[:, t * P:(t + 1) * P], comp2[:],
                                            start=True, stop=True)
                last.then_inc(s_qst, 1)

            def head_spread(i, sq, bank):
                if not isinstance(i, int) or i > H + 2:
                    pe.wait_ge(s_on, i - (H + 2))
                pe.wait_ge(s_qrs, i * 2 + 2)
                if not at_start(i):
                    pe.wait_ge(s_qn, i)
                spread(bank, lambda t: sq[:, t * P:(t + 1) * P], s_qbc)

            for i in range(H + 2):
                wait_acc(U_K + i)
                wait_slab(S_K + i)
                inp = I_KV if i < H else I_Q
                product((U_K + i) % ACC, S_K + i, operand(inp), range(0, 4), chunks_of(I_Q) if i == H else None)
                if i >= 1:
                    head_sums(i - 1, sq_qk[(i - 1) % 2], STAT, 0)
                product((U_K + i) % ACC, S_K + i, operand(inp), range(4, KC), chunks_of(I_Q) if i == H else None).then_inc(s_used, 1)
                if i >= 1:
                    head_spread(i - 1, sq_qk[(i - 1) % 2], BC)
            head_sums(H + 1, sq_qk[1], STAT, 0)
            head_spread(H + 1, sq_qk[1], BC)
            pe.wait_ge(s_qn, H + 2)
            pe.wait_ge(s_acc, U_WO)

            def scores(h, i, b):
                if i == 0:
                    pe.wait_ge(s_qlo, h * 2 + 2)
                if not (at_start(h) and i < 2):
                    pe.wait_ge(s_exp, h * 8 + 2 * (i - 1))
                kw = max((i + 1) * P, 2 * P)
                for c in range(2):
                    rows = slice(c * HD, (c + 1) * HD)
                    bank = 2 * (i % 2) + c
                    for j, (q, k) in enumerate(((q_hi, k_hi), (q_hi, k_lo), (q_lo, k_hi))):
                        nc.tensor.matmul(ps[:, bank, 0:kw], q[b][rows, i * P:(i + 1) * P], k[b][rows, 0:kw],
                                         start=(j == 0), stop=False)
                    last = nc.tensor.matmul(ps[:, bank, i * P:(i + 1) * P], identb[:], maskb[:], start=False, stop=True)
                last.then_inc(s_S, 1)

            def weights_T(h, i):
                pe.wait_ge(s_at, h * 4 + i + 1)
                if not (at_start(h) and i == 0):
                    pe.wait_ge(s_Thi, h * 4 + i)
                    pe.wait_ge(s_Tlo, h * 4 + i)
                for j in range(i + 1):
                    last = nc.tensor.transpose(ps[:, B_AT, j * P:(j + 1) * P], p_buf[i % 2][:, 0, j * P:(j + 1) * P], ident[:])
                last.then_inc(s_T, 1)

            def values(h, p):
                pe.wait_ge(s_Thi, h * 4 + 2 * p + 2)
                pe.wait_ge(s_Tlo, h * 4 + 2 * p + 2)
                if p == 0:
                    pe.wait_ge(s_vlo, h + 1)
                    if not at_start(h):
                        pe.wait_ge(s_oc, h * 2)
                nj = 2 * p + 2
                for j in range(nj):
                    for i, (v, a) in enumerate(((v_hi, at_hi), (v_hi, at_lo), (v_lo, at_hi))):
                        last = nc.tensor.matmul(ps[:, B_O, p * 256:(p + 1) * 256], v[:, j, :], a[p][:, j, :],
                                                start=(j == 0 and i == 0), stop=(j == nj - 1 and i == 2))
                last.then_inc(s_pv, 1)

            def out_sums(h):
                pe.wait_ge(s_oc, h * 2 + 2)
                for t in range(TB):
                    last = nc.tensor.matmul(ps[:, B_BC, 2 * t:2 * t + 2], o_sq[:, t * P:(t + 1) * P], ones2[:],
                                            start=True, stop=True)
                last.then_inc(s_ost, 1)

            def out_spread(h):
                pe.wait_ge(s_ors, h + 1)
                spread(B_BC, lambda t: ors[:, 2 * t:2 * t + 1].to_broadcast([P, P]), s_obc)

            def project(h, b, ks):
                if 0 in ks:
                    pe.wait_ge(s_wlo, h + (S_Q + 1))
                    if not (isinstance(h, int) and h == HEAD_AHEAD):
                        pe.wait_ge(s_qms, h * 2 + 2 * H)
                return product(B_Q, S_Q + b, operand(I_Q), ks)

            def head(h, b, prev, nxt, far):
                scores(h, 2, b)
                if far is not None:
                    project(far, b, range(0, 3))
                if prev is not None:
                    values(prev, 1)
                    if nxt is not None:
                        head_spread(nxt + H, sq_qk[0], B_BC)
                weights_T(h, 0)
                scores(h, 3, b)
                if far is not None:
                    project(far, b, range(3, 6))
                if prev is not None:
                    if nxt is not None:
                        pe.wait_ge(s_qn, nxt + (H + 1))
                    else:
                        pe.wait_ge(s_on, prev)
                    out_sums(prev)
                weights_T(h, 1)
                if nxt is not None:
                    scores(nxt, 0, 1 - b)
                if far is not None:
                    project(far, b, range(6, KC)).then_inc(s_used, 1)
                values(h, 0)
                weights_T(h, 2)
                if nxt is not None:
                    scores(nxt, 1, 1 - b)
                if prev is not None:
                    out_spread(prev)
                if far is not None:
                    pe.wait_ge(s_qc, far + (H + 1))
                    head_sums(far + H, sq_qk[0], B_Q, 8)
                weights_T(h, 3)

            scores(0, 0, 0)
            scores(0, 1, 0)
            heads(pe, head)
            values(H - 1, 1)
            pe.wait_ge(s_on, H - 1)
            out_sums(H - 1)
            out_spread(H - 1)

            for m in range(KC):
                dense(S_WO + m, U_WO + m, I_O, m == 0)
            mlp(1, S_MLP1, U_MLP1, I_M1, NORM_M1)

        @block.scalar
        def _(act):
            with nc.allow_non_contiguous_dma(reason="gains: one float a feature"):
                def par(dst, src):
                    act.dma_start(dst, src).then_inc(s_par, 16)
                par(gains[:, g_a, :], a_norm.rearrange("l (k p) -> p (l k)", p=P))
                par(gains[:, g_m0:g_m1 + 1, :], mlp_norm.rearrange("l (k p) -> p l k", p=P))
                par(gains[:, g_kv, :], kv_norm.rearrange("(k p) -> p k", p=P))
                par(gains[:, g_b, :], b_norm.rearrange("l (k p) -> p (l k)", p=P))
                par(conv[:, :, :], a_conv.rearrange("l w (k p) -> p (l w) k", p=P))
                for c in range(2):
                    par(hg[c * HD:(c + 1) * HD, 0:1], q_norm.rearrange("l d -> d l"))
                    par(hg[c * HD:(c + 1) * HD, 1:2], k_norm.rearrange("(d o) -> d o", o=1))
                par(hg[:, 2:3], sub_norm.rearrange("l d -> d l"))
                for i, v in enumerate((lam_q1, lam_k1, lam_q2, lam_k2)):
                    par(lamv[:, i, :], v.to_broadcast([P, HD]))

            def split(n, off=0):
                act.wait_ge(s_raw[n % RAW], off * (16 // RAW) + 16 * (n // RAW + 1))
                if freed(n):
                    act.wait_ge(s_used, off + freed(n))
                nc.scalar.activation(w_hi[:, slot(n), :], w_raw[:, n % RAW, :], ACT.Copy).then_inc(s_whi, 1)

            def chunk_hi(i, m, g):
                nc.scalar.activation(h_of[i][:, 0, m, :], xT[:, m, :], ACT.Copy, scale=gains[:, g, m:m + 1]).then_inc(s_hi, 1)

            def square(i, m):
                if 8 * i + m >= 2:
                    act.wait_ge(s_add, 8 * i + m - 1)
                nc.scalar.activation(sqb[m % 2], xT[:, m, :], ACT.Square).then_inc(s_sq, 1)

            def row_scales(count):
                act.wait_ge(s_nbc, count)
                nc.scalar.activation(rB[:], ps[:, BC, :], ACT.Copy).then_inc(s_rB, 1)

            for t in range(TB):
                act.wait_ge(s_xt, 2 * t + 2)
                nc.scalar.activation(xT[:, 4:8, t * P:(t + 1) * P],
                                     ps[:, 2 * t + 1, :].rearrange("p (k q) -> p k q", k=4), ACT.Copy).then_inc(s_xa, 1)
            act.wait_ge(s_par, 16 * 14)
            act.wait_ge(s_xd, TB)
            act.wait_ge(s_xa, TB)
            split(0)
            for m in range(KC):
                chunk_hi(I_A, m, g_a)
                square(NORM_A, m)
                if m == 3:
                    split(1)
            act.wait_ge(s_cst, 7)
            nc.scalar.activation(lams[:, 2:4], lams[:, 0:2], ACT.Exp).then_inc(s_lam, 1)
            for n in range(N_IN):
                split(n + AHEAD)
                if n == 1:
                    row_scales(1)
                if n % 3 == 2:
                    j = n // 3
                    act.wait_ge(s_mix, 9 * (j + 1))
                    nc.scalar.activation(h2[:, 0, j, :], mix[5 + j % 2], ACT.Copy).then_inc(s_hi, 1)
            for m in range(KC):
                split(S_OUT + m + AHEAD)
                act.wait_ge(s_acc, U_OUT + m + 1)
                chunk_hi(I_M0, m, g_m0)
                square(NORM_M0, m)

            def mlp(layer, base, ubase, count, after):
                def quarter(q, first=False, last=False):
                    for j in range(8):
                        split(base + j + AHEAD, q * 16)
                        if first and j == 0:
                            pass
                        if first and j == 1:
                            row_scales(count)
                        for jj in ((0, 1) if j == 1 else () if j == 0 else (j,)):
                            act.wait_ge(s_r, q * 8 + (32 * layer + jj + 1))
                            nc.scalar.activation(ah[:, jj, :], mix[jj % 2], ACT.Square).then_inc(s_ahi, 1)
                    for m in range(8):
                        n = base + 8 + m + AHEAD
                        if not (last and n + q * 16 >= S_END):
                            split(n, q * 16)
                        if last:
                            after(m)

                quarter(0, first=True)
                with act.Fori(1, NQ - 1) as q:
                    quarter(q)
                quarter(NQ - 1, last=True)

            def after0(m):
                act.wait_ge(s_acc, U_MLP0 + 56 + m + 1)
                chunk_hi(I_KV, m, g_kv)
                square(NORM_B, m)

            mlp(0, S_MLP0, U_MLP0, 2, after0)
            for n in range(8):
                split(S_V + n + AHEAD)
                chunk_hi(I_Q, n, g_b)
            def square_qk(i, src, sq, count):
                act.wait_ge(s_qc, count)
                if i >= 2:
                    act.wait_ge(s_qbc, i - 1)
                nc.scalar.activation(sq, src, ACT.Square).then_inc(s_qsq, 1)

            for i in range(H + 2):
                if i != H:
                    split(S_K + i + AHEAD - (i > H))
                square_qk(i, raw_qk[i % 2], sq_qk[i % 2], i + 1)

            def copy_q(h):
                act.wait_ge(s_used, h + (S_Q + 1))
                act.wait_ge(s_qhi, h * 2)
                act.wait_ge(s_qlo, h * 2)
                nc.scalar.activation(raw_qk[0], ps[:, B_Q, :], ACT.Copy).then_inc(s_qc, 1)
                act.wait_ge(s_qbc, h + H)
                nc.scalar.activation(sq_qk[0], ps[:, B_Q, :], ACT.Square).then_inc(s_qsq, 1)

            def q_hi_part(h, b, raw):
                act.wait_ge(s_qn, h + (H + 1))
                nc.scalar.activation(q_hi[b], raw, ACT.Copy).then_inc(s_qhi, 1)

            def k_hi_part(h, b):
                nc.scalar.activation(k_hi[b], kv[:, bass.ds(h, 1), :].rearrange("p a b -> p (a b)"), ACT.Copy).then_inc(s_qhi, 1)

            act.wait_ge(s_used, S_V)
            act.wait_ge(s_qn, H)
            for h in range(2):
                k_hi_part(h, h)
                q_hi_part(h, h, raw_qk[h])

            def exps(h, i):
                act.wait_ge(s_mx, h * 4 + i + 1)
                if not (at_start(h) and i < 2):
                    act.wait_ge(s_T, h * 4 + i - 1)
                kw = (i + 1) * P
                for c in range(2):
                    nc.scalar.activation(p_buf[i % 2][:, c, 0:kw], ps[:, 2 * (i % 2) + c, 0:kw], ACT.Exp,
                                         bias=nmax[:, i % 2, c:c + 1], accum_out=rsum[:, i % 2, c:c + 1]).then_inc(s_exp, 1)

            def weights_hi(h, i):
                act.wait_ge(s_T, h * 4 + i + 1)
                if not at_start(h):
                    act.wait_ge(s_pv, h * 2 + i // 2 - 1)
                nc.scalar.activation(at_hi[i // 2][:, 0:i + 1, (i % 2) * P:(i % 2 + 1) * P],
                                     ps[:, B_AT, 0:(i + 1) * P].rearrange("p (j q) -> p j q", j=i + 1), ACT.Copy).then_inc(s_Thi, 1)

            def v_split(h):
                if not at_start(h):
                    act.wait_ge(s_pv, h * 2)
                nc.scalar.activation(v_hi, v_all[:, :, bass.ds(h * P, P)], ACT.Copy).then_inc(s_vhi, 1)

            def copy_o(h):
                act.wait_ge(s_pv, h * 2 + 2)
                if at_start(h):
                    act.wait_ge(s_qlo, 4)
                    act.wait_ge(s_qbc, H + 2)
                else:
                    act.wait_ge(s_hi, h + 8 * I_O)
                    act.wait_ge(s_lo, h + 8 * I_O)
                    act.wait_ge(s_ost, h)
                nc.scalar.activation(o_sb, ps[:, B_O, :], ACT.Copy).then_inc(s_oc, 1)
                nc.scalar.activation(o_sq, ps[:, B_O, :], ACT.Square).then_inc(s_oc, 1)

            def out_hi(h):
                act.wait_ge(s_on, h + 1)
                nc.scalar.activation(h2[:, 0, bass.ds(h, 1), :].rearrange("p a b -> p (a b)"), o_sb, ACT.Copy).then_inc(s_hi, 1)

            def next_slab(h, b):
                n = S_Q + HEAD_AHEAD + 1 + b
                off = h - b
                act.wait_ge(s_raw[n % RAW], off * 8 + 16 * (n // RAW + 1))
                act.wait_ge(s_used, off + n - 1)
                nc.scalar.activation(w_hi[:, n % 2, :], w_raw[:, n % RAW, :], ACT.Copy).then_inc(s_whi, 1)

            def head(h, b, prev, nxt, far):
                new_q = prev is not None and nxt is not None
                exps(h, 1)
                if new_q:
                    k_hi_part(nxt, 1 - b)
                if prev is not None:
                    copy_o(prev)
                weights_hi(h, 0)
                exps(h, 2)
                if new_q:
                    q_hi_part(nxt, 1 - b, raw_qk[0])
                v_split(h)
                weights_hi(h, 1)
                if nxt is not None:
                    next_slab(h, b)
                exps(h, 3)
                weights_hi(h, 2)
                if nxt is not None:
                    exps(nxt, 0)
                if far is not None:
                    copy_q(far)
                weights_hi(h, 3)
                if prev is not None:
                    out_hi(prev)

            exps(0, 0)
            heads(act, head)
            copy_o(H - 1)
            out_hi(H - 1)

            for m in range(KC):
                split(S_WO + m + AHEAD)
                act.wait_ge(s_acc, U_WO + m + 1)
                chunk_hi(I_M1, m, g_m1)
                square(NORM_M1, m)

            def after1(m):
                if m >= 1:
                    copy_out(m - 1)

            def copy_out(m):
                act.wait_ge(s_fT, m + 1)
                nc.scalar.activation(kv[:, m, :], ps[:, BC + m % 2, :], ACT.Copy).then_inc(s_fc, 1)

            mlp(1, S_MLP1, U_MLP1, 3, after1)
            copy_out(KC - 1)

        @block.vector
        def _(dve):
            V = nc.vector
            mixed = [0]

            def mix_step(ins, wait=True):
                mixed[0] += 1
                ins.then_inc(s_mix, 1)
                dve.wait_ge(s_mix, mixed[0])

            def split(n, off=0):
                dve.wait_ge(s_whi, off + n + 1)
                V.tensor_tensor(w_lo[:, slot(n), :], w_raw[:, n % RAW, :], w_hi[:, slot(n), :].bitcast(F32),
                                ALU.subtract).then_inc(s_wlo, 1)

            def chunk_lo(i, m, g):
                dve.wait_ge(s_hi, 8 * i + m + 1)
                V.scalar_tensor_tensor(h_of[i][:, 1, m, :], xT[:, m, :], gains[:, g, m:m + 1],
                                       h_of[i][:, 0, m, :].bitcast(F32), ALU.mult, ALU.subtract).then_inc(s_lo, 1)

            def residual(n, u, m, off=0):
                dve.wait_ge(s_used, off + n + 1)
                V.tensor_tensor(xT[:, m, :], ps[:, u % ACC, :], xT[:, m, :], ALU.add).then_inc(s_acc, 1)

            def mean_squares(i):
                dve.wait_ge(s_nst, i + 1)
                V.tensor_scalar(nms[:, i, :], ps[:, STAT, 0:2 * TB].rearrange("p (t c) -> p t c", c=2)[:, :, 0], 1.0 / D, EPS,
                                ALU.mult, ALU.add).then_inc(s_nms, 1)

            V.memset(ones2[:], 1.0).then_inc(s_cst, 1)
            V.memset(comp2[:], 0.0).then_inc(s_cst, 1)
            dve.wait_ge(s_cst, 2)
            V.memset(comp2[0:HD, 0:1], 1.0).then_inc(s_cst, 1)
            V.memset(comp2[HD:P, 1:2], 1.0).then_inc(s_cst, 1)
            V.memset(mix[2][:, 0:2], 0.0).then_inc(s_mix, 1)
            mixed[0] += 1
            dve.wait_ge(s_zero, 3)
            V.tensor_copy(identb[:], ident[:]).then_inc(s_cst, 1)
            for t in range(TB):
                dve.wait_ge(s_xt, 2 * t + 1)
                V.tensor_copy(xT[:, 0:4, t * P:(t + 1) * P],
                              ps[:, 2 * t, :].rearrange("p (k q) -> p k q", k=4)).then_inc(s_xd, 1)
            dve.wait_ge(s_par, 16 * 14)
            dve.wait_ge(s_xd, TB)
            dve.wait_ge(s_xa, TB)
            split(0)
            for m in range(KC):
                chunk_lo(I_A, m, g_a)
                if m == 3:
                    split(1)
            for i in range(2):
                V.tensor_tensor_reduce(out=lamp[:], in0=lamv[:, 2 * i, :], in1=lamv[:, 2 * i + 1, :], scale=1.0, scalar=0.0,
                                       op0=ALU.mult, op1=ALU.add, accum_out=lams[:, i:i + 1]).then_inc(s_cst, 1)
                dve.wait_ge(s_cst, 6 + i)
            for i, c in enumerate((HD ** -0.5, 1.0, 1.0 - LAM_INIT)):
                V.tensor_scalar(hgs[:, i:i + 1], hg[:, i:i + 1], c, None, ALU.mult).then_inc(s_cst, 1)
            dve.wait_ge(s_lam, 1)
            V.tensor_tensor(lams[:, 4:5], lams[:, 3:4], lams[:, 2:3], ALU.subtract).then_inc(s_cst, 1)
            dve.wait_ge(s_cst, 11)
            V.tensor_scalar(lams[:, 5:6], lams[:, 4:5], -LAM_INIT, None, ALU.add).then_inc(s_cst, 1)
            mean_squares(NORM_A)

            cr, u, t0, br = mix[0], work[:, U0:U0 + T + 2], mix[1], mix[4]
            for n in range(N_IN):
                split(n + AHEAD)
                if n == 0:
                    dve.wait_ge(s_rB, 1)
                j = n // 3
                acc = ps[:, (U_IN + n) % ACC, :]
                dve.wait_ge(s_used, n + 1)
                if n % 3 == 0:
                    V.tensor_tensor(cr, acc, rB[:], ALU.mult).then_inc(s_acc, 1)
                    dve.wait_ge(s_acc, n + 1)
                    mix_step(V.tensor_tensor(cr, cr, rB[:], ALU.mult))
                elif n % 3 == 1:
                    V.tensor_tensor(u[:, 2:T + 2], acc, cr, ALU.mult).then_inc(s_acc, 1)
                    dve.wait_ge(s_acc, n + 1)
                    mix_step(V.tensor_scalar(t0, u[:, 0:T], conv[:, 0, j:j + 1], None, ALU.mult))
                    mix_step(V.scalar_tensor_tensor(t0, u[:, 1:T + 1], conv[:, 1, j:j + 1], t0, ALU.mult, ALU.add))
                    mix_step(V.scalar_tensor_tensor(t0, u[:, 2:T + 2], conv[:, 2, j:j + 1], t0, ALU.mult, ALU.add))
                else:
                    V.tensor_tensor(br, acc, rB[:], ALU.mult).then_inc(s_acc, 1)
                    dve.wait_ge(s_acc, n + 1)
                    if j >= 2:
                        dve.wait_ge(s_hi, 8 * I_Z + j - 1)
                    z = mix[5 + j % 2]
                    V.tensor_tensor(z, br, t0, ALU.mult).then_inc(s_mix, 9 * (j + 1) - mixed[0])
                    mixed[0] = 9 * (j + 1)
                    dve.wait_ge(s_mix, mixed[0])
                    dve.wait_ge(s_hi, 8 * I_Z + j + 1)
                    V.tensor_tensor(h2[:, 1, j, :], z, h2[:, 0, j, :].bitcast(F32), ALU.subtract).then_inc(s_lo, 1)
            for m in range(KC):
                split(S_OUT + m + AHEAD)
                residual(S_OUT + m, U_OUT + m, m)
                dve.wait_ge(s_acc, U_OUT + m + 1)
                chunk_lo(I_M0, m, g_m0)

            def mlp(layer, base, ubase, norm, scales, after):
                def unit(j, q):
                    c = 32 * layer + j + 1
                    dve.wait_ge(s_used, q * 16 + base + j + 1)
                    if not (at_start(q) and layer == 0 and j < 2):
                        dve.wait_ge(s_ahi, q * 8 + c - 2)
                    V.scalar_tensor_tensor(mix[j % 2], ps[:, (ubase + j) % ACC, :], 0.0, rB[:], ALU.max, ALU.mult).then_inc(s_r, 1)
                    dve.wait_ge(s_r, q * 8 + c)
                    V.tensor_tensor(mix[2], mix[j % 2], mix[j % 2], ALU.mult).then_inc(s_acc, 1)
                    dve.wait_ge(s_acc, q * 16 + ubase + j + 1)
                    dve.wait_ge(s_ahi, q * 8 + c)
                    V.tensor_tensor(ah[:, 8 + j, :], mix[2], ah[:, j, :].bitcast(F32), ALU.subtract).then_inc(s_alo, 1)

                def quarter(q, first=False, last=False):
                    for j in range(8):
                        split(base + j + AHEAD, q * 16)
                        if first and j == 0:
                            mean_squares(norm)
                        if first and j == 1:
                            dve.wait_ge(s_rB, scales)
                        for jj in ((0, 1) if j == 1 else () if j == 0 else (j,)):
                            unit(jj, q)
                    for m in range(8):
                        n = base + 8 + m
                        if not (last and n + AHEAD + q * 16 >= S_END):
                            split(n + AHEAD, q * 16)
                        residual(n, ubase + 8 + m, m, q * 16)
                        if last:
                            after(m)

                quarter(0, first=True)
                with dve.Fori(1, NQ - 1) as q:
                    quarter(q)
                quarter(NQ - 1, last=True)

            def after0(m):
                dve.wait_ge(s_acc, U_MLP0 + 56 + m + 1)
                chunk_lo(I_KV, m, g_kv)

            mlp(0, S_MLP0, U_MLP0, NORM_M0, 2, after0)

            for n in range(8):
                split(S_V + n + AHEAD)
                if n == 0:
                    mean_squares(NORM_B)
                chunk_lo(I_Q, n, g_b)
                if n % 4 == 3:
                    g = n // 4
                    dve.wait_ge(s_nrc, NORM_B + 1)
                    dve.wait_ge(s_used, S_V + n + 1)
                    for t in range(TB):
                        V.tensor_scalar(v_all[:, t, g * T:(g + 1) * T], ps[:, (U_V + t) % ACC, :], rcol[:, NORM_B, t:t + 1], None,
                                        ALU.mult).then_inc(s_acc, 1)
            V.scalar_tensor_tensor(r2[:], rcol[:, NORM_B, :], 1.0 / HD, rcol[:, NORM_B, :], ALU.mult, ALU.mult).then_inc(s_cst, 1)
            dve.wait_ge(s_cst, 13)

            def head_ms(i, b, bank, at):
                dve.wait_ge(s_qst, i + 1)
                if not (isinstance(i, int) and i < 2):
                    dve.wait_ge(s_qrs, i * 2 - 3)
                V.tensor_tensor(qms[:, b, :].rearrange("p (t c) -> p t c", c=2),
                                ps[:, bank, at:at + 8].rearrange("p (t c) -> p t c", c=2),
                                r2[:].unsqueeze(2).to_broadcast([P, TB, 2]), ALU.mult).then_inc(s_qms, 1)
                dve.wait_ge(s_qms, i * 2 + 1)
                V.tensor_scalar(qms[:, b, :], qms[:, b, :], EPS, None, ALU.add).then_inc(s_qms, 1)

            def k_norm_step(i):
                dve.wait_ge(s_qbc, i + 1)
                V.scalar_tensor_tensor(kv[:, i, :] if i < H else raw_qk[i % 2], raw_qk[i % 2], hgs[:, 1:2] if i < H else hgs[:, 0:1],
                                       ps[:, BC, :], ALU.mult, ALU.mult).then_inc(s_qn, 1)

            for i in range(H + 2):
                if i != H:
                    split(S_K + i + AHEAD - (i > H))
                if i >= 1:
                    head_ms(i - 1, (i - 1) % 2, STAT, 0)
                dve.wait_ge(s_used, S_K + i + 1)
                if i >= 2:
                    dve.wait_ge(s_qn, i - 1)
                V.tensor_copy(raw_qk[i % 2], ps[:, (U_K + i) % ACC, :]).then_inc(s_acc, 1)
                dve.wait_ge(s_acc, U_K + i + 1)
                V.memset(lamp[:, 0:1], 0.0).then_inc(s_qc, 1)
                if i >= 1:
                    k_norm_step(i - 1)
            head_ms(H + 1, 1, STAT, 0)
            k_norm_step(H + 1)

            def normalise_q(i):
                dve.wait_ge(s_qbc, i + 1)
                V.scalar_tensor_tensor(raw_qk[0], raw_qk[0], hgs[:, 0:1], ps[:, B_BC, :], ALU.mult, ALU.mult).then_inc(s_qn, 1)

            def row_max(h, i):
                b = i % 2
                kw = (i + 1) * P
                dve.wait_ge(s_S, h * 4 + i + 1)
                if not (at_start(h) and i < 2):
                    dve.wait_ge(s_exp, h * 8 + 2 * i - 2)
                V.tensor_reduce(nmax[:, b, :], ps[:, 2 * b:2 * b + 2, 0:kw], AX_X, ALU.max, negate=True).then_inc(s_mx, 1)

            def weights(h, i):
                b = i % 2
                kw = (i + 1) * P
                p1, p2 = p_buf[b][:, 0, 0:kw], p_buf[b][:, 1, 0:kw]
                dve.wait_ge(s_exp, h * 8 + 2 * i + 2)
                V.reciprocal(rinv[:, b, :], rsum[:, b, :]).then_inc(s_sc, 1)
                dve.wait_ge(s_sc, h * 8 + 2 * i + 1)
                V.tensor_scalar(p2, p2, rinv[:, b, 1:2], lams[:, 5:6], ALU.mult, ALU.mult).then_inc(s_sc, 1)
                dve.wait_ge(s_sc, h * 8 + 2 * i + 2)
                V.scalar_tensor_tensor(p1, p1, rinv[:, b, 0:1], p2, ALU.mult, ALU.add).then_inc(s_at, 1)

            def weights_lo(h, i):
                dve.wait_ge(s_Thi, h * 4 + i + 1)
                cols = slice((i % 2) * P, (i % 2 + 1) * P)
                V.tensor_tensor(at_lo[i // 2][:, 0:i + 1, cols], ps[:, B_AT, 0:(i + 1) * P].rearrange("p (j q) -> p j q", j=i + 1),
                                at_hi[i // 2][:, 0:i + 1, cols].bitcast(F32), ALU.subtract).then_inc(s_Tlo, 1)

            def out_ms(h):
                dve.wait_ge(s_ost, h + 1)
                if not at_start(h):
                    dve.wait_ge(s_ors, h)
                V.tensor_scalar(oms[:], ps[:, B_BC, 0:8], 1.0 / P, EPS, ALU.mult, ALU.add).then_inc(s_oms, 1)

            def out_norm(h):
                dve.wait_ge(s_obc, h + 1)
                V.scalar_tensor_tensor(o_sb, o_sb, hgs[:, 2:3], ps[:, B_BC, :], ALU.mult, ALU.mult).then_inc(s_on, 1)

            def next_slab(h, b):
                n = S_Q + HEAD_AHEAD + 1 + b
                dve.wait_ge(s_whi, h + (n - b + 1))
                V.tensor_tensor(w_lo[:, n % 2, :], w_raw[:, n % RAW, :], w_hi[:, n % 2, :].bitcast(F32),
                                ALU.subtract).then_inc(s_wlo, 1)

            def head(h, b, prev, nxt, far):
                weights(h, 0)
                row_max(h, 2)
                if prev is not None and nxt is not None:
                    normalise_q(nxt + H)
                weights_lo(h, 0)
                weights(h, 1)
                row_max(h, 3)
                weights_lo(h, 1)
                if prev is not None:
                    out_ms(prev)
                weights(h, 2)
                if nxt is not None:
                    row_max(nxt, 0)
                    next_slab(h, b)
                weights_lo(h, 2)
                weights(h, 3)
                if nxt is not None:
                    row_max(nxt, 1)
                if prev is not None:
                    out_norm(prev)
                if far is not None:
                    head_ms(far + H, b, B_Q, 8)
                weights_lo(h, 3)

            row_max(0, 0)
            row_max(0, 1)
            heads(dve, head)
            out_ms(H - 1)
            out_norm(H - 1)

            for m in range(KC):
                split(S_WO + m + AHEAD)
                residual(S_WO + m, U_WO + m, m)
                dve.wait_ge(s_acc, U_WO + m + 1)
                chunk_lo(I_M1, m, g_m1)
            mlp(1, S_MLP1, U_MLP1, NORM_M1, 3, lambda m: None)


_INS = ["x", "a_norm", "a_w_in", "a_conv", "a_w_out", "kv_norm", "w_kv", "k_norm", "b_norm", "w_q", "q_norm",
        "lam_q1", "lam_k1", "lam_q2", "lam_k2", "sub_norm", "w_o", "mlp_norm", "w_up", "w_down"]


def kernel(**inputs):
    import numpy as np
    import concourse.bacc as bacc
    from concourse.bass_utils import run_bass_kernel_spmd

    nc = bacc.Bacc("TRN2", target_bir_lowering=False, num_devices=1)
    arrays, args = {}, []
    for name in _INS:
        a = np.ascontiguousarray(inputs[name])
        arrays[f"in_{name}"] = a
        args.append(nc.dram_tensor(f"in_{name}", a.shape, mybir.dt.from_np(a.dtype), kind="ExternalInput").ap())
    out = nc.dram_tensor("out_x", (1, T, D), F32, kind="ExternalOutput").ap()
    build(nc, *args, out)
    r = run_bass_kernel_spmd(nc, [arrays], core_ids=[0])
    return r.results[0]["out_x"]
```

```python
import math
from contextlib import ExitStack

import concourse.bass as bass
from concourse import mybir


F32 = mybir.dt.float32
F32R = mybir.dt.float32r
BF16 = mybir.dt.bfloat16
ALU = mybir.AluOpType
ACT = mybir.ActivationFunctionType
AX_X = mybir.AxisListType.X

P = 128
T = 512
TB = T // P
D = 1024
KC = D // P
NQ = 4
H = 8
HD = 64
EPS = 1e-6
NEG = -1e30
LAM_INIT = 0.8 - 0.6 * math.exp(-0.3 * 1)
SLAB = 1024
N_PAR = 12

RAW = 2
RING = 4
AHEAD = 2
ACC = 4
BC, STAT = 6, 7
B_Q, B_AT, B_O, B_BC = 4, 5, 6, 7
HEAD_AHEAD = 2
Q_BANK = (B_AT, B_Q)
KV_BANKS = 6
K_T_AFTER = 7
WO_BANK = (B_Q, 1, 2, 3, 0, 1, 2, 3)
WO_SPLITS = ((4, 5), (), (6,), (7,), (), (), (8,), (), (9,))

N_IN, N_OUT = 24, 8
S_IN = 0
S_OUT = S_IN + N_IN
S_MLP0 = S_OUT + N_OUT
S_KV = S_MLP0 + NQ * 16
S_Q = S_KV + 16
S_WO = S_Q + H
S_MLP1 = S_WO + 8
S_END = S_MLP1 + NQ * 16

U_IN, U_OUT, U_MLP0, U_KV, U_WO, U_MLP1 = 0, 24, 32, 96, 112, 120

I_A, I_Z, I_M0, I_KV, I_Q, I_O, I_M1 = range(7)
NORM_A, NORM_M0, NORM_B, NORM_M1 = range(4)


def slot(n):
    return (n % 2) if S_Q <= n < S_WO else n % RING


def freed(n):
    if S_Q + 2 <= n < S_WO + 2:
        return n - 1
    return n - RING + 1 if n >= RING else 0


def at_start(i):
    return isinstance(i, int) and i == 0


def heads(engine, head):
    head(0, 0, None, 1, 2)
    head(1, 1, 0, 2, 3)
    with engine.Fori(0, (H - 4) // 2) as it:
        head(it * 2 + 2, 0, it * 2 + 1, it * 2 + 3, it * 2 + 4)
        head(it * 2 + 3, 1, it * 2 + 2, it * 2 + 4, it * 2 + 5)
    head(H - 2, 0, H - 3, H - 1, None)
    head(H - 1, 1, H - 2, None, None)


def build(nc, x, a_norm, a_w_in, a_conv, a_w_out, kv_norm, w_kv, k_norm, b_norm, w_q, q_norm,
          lam_q1, lam_k1, lam_q2, lam_k2, sub_norm, w_o, mlp_norm, w_up, w_down, out):
    with ExitStack() as ctx:
        def sb(name, shape, dt=F32):
            return ctx.enter_context(nc.sbuf_tensor(name, shape, dt))

        def sem(name):
            return ctx.enter_context(nc.semaphore(name))

        xT = sb("xT", [P, KC, T])
        h1 = sb("h1", [P, 2, KC, T], F32R)
        h2 = sb("h2", [P, 2, KC, T], F32R)
        ah = sb("ah", [P, 16, T], F32R)
        kv = sb("kv", [P, 16, T])
        w_raw = sb("w_raw", [P, RAW, SLAB])
        w_hi = sb("w_hi", [P, RING, SLAB], F32R)
        w_lo = sb("w_lo", [P, RING, SLAB], F32R)
        rB = sb("rB", [P, T])
        work = sb("work", [P, 4096])
        sqsum = work[:, 3584:4096]
        ident = sb("ident", [P, P])
        identb = sb("identb", [P, P], BF16)
        maskb = sb("maskb", [P, P], BF16)
        comp2 = sb("comp2", [P, 2])
        ones2 = sb("ones2", [P, 2])
        mhalf = sb("mhalf", [P, 32])
        gains = sb("gains", [P, 5, KC])
        conv = sb("conv", [P, 3, KC])
        hg = sb("hg", [P, 3])
        hgs = sb("hgs", [P, 3])
        lamv = sb("lamv", [P, 4, HD])
        lamp = sb("lamp", [P, HD])
        lams = sb("lams", [P, 8])
        nms = sb("nms", [P, 4, TB])
        rcol = sb("rcol", [P, 4, TB])
        r2 = sb("r2", [P, TB])
        qms = sb("qms", [P, 2, 8])
        qpw = sb("qpw", [P, 8])
        k_ms = sb("k_ms", [P, 2, 32])
        k_rs = sb("k_rs", [P, 2, 32])
        q_scale = sb("q_scale", [P, 2, 2 * TB])
        oms = sb("oms", [P, 8])
        ors = sb("ors", [P, 8])
        nmax = sb("nmax", [P, 2, 2])
        bias = sb("bias", [P, 2, 2])
        rsum = sb("rsum", [P, 2, 2])
        rinv = sb("rinv", [P, 2, 2])
        ps = ctx.enter_context(nc.psum_tensor("ps", [P, 8, T], F32))

        g_a, g_m0, g_m1, g_kv, g_b = range(5)
        mix = [work[:, i * T:(i + 1) * T] for i in range(7)]
        U0 = 2 * T
        sqb = [work[:, 6 * T - 1024 + i * T:6 * T - 1024 + (i + 1) * T] for i in range(2)]
        p_buf = [work[:, (4 + 2 * i) * T:(6 + 2 * i) * T].rearrange("p (c k) -> p c k", c=2) for i in range(2)]
        at_hi = [ah[:, 0, :].rearrange("p (j q) -> p j q", j=2), ah[:, 2:4, :].rearrange("p a (j q) -> p (a j) q", j=2)]
        at_lo = [ah[:, 1, :].rearrange("p (j q) -> p j q", j=2), ah[:, 4:6, :].rearrange("p a (j q) -> p (a j) q", j=2)]
        q_hi, q_lo = [ah[:, 6 + 2 * b, :] for b in range(2)], [ah[:, 7 + 2 * b, :] for b in range(2)]
        k_hi, k_lo = [ah[:, 10 + 2 * b, :] for b in range(2)], [ah[:, 11 + 2 * b, :] for b in range(2)]
        v_hi, v_lo = ah[:, 14, :].rearrange("p (t e) -> p t e", t=TB), ah[:, 15, :].rearrange("p (t e) -> p t e", t=TB)
        v_all = kv[:, 8:16, :].rearrange("p a b -> p (a b)").rearrange("p (t f) -> p t f", t=TB)
        x_tok = kv[:, 0:8, :].rearrange("p a b -> p (a b)").rearrange("p (t f) -> p t f", t=TB)
        k_tok = [[kv[:, 4 * g:4 * g + 4, t * P:(t + 1) * P] for t in range(TB)] for g in range(2)]
        k_sq = [work[:, i * T:(i + 1) * T] for i in range(2)]
        sq_q = [work[:, T:2 * T], work[:, 3 * T:4 * T]]
        o_sb, o_sq = work[:, 2 * T:3 * T], work[:, 3 * T:4 * T]
        h_of = [h1, h2, h1, h2, h1, h2, h1]

        s_x = [sem(f"s_x{t}") for t in range(TB)]
        s_gain_a = sem("s_gain_a")
        s_conv = sem("s_conv")
        s_par = sem("s_par")
        s_raw = [sem(f"s_raw{i}") for i in range(RAW)]
        s_whi = sem("s_whi")
        s_wlo = sem("s_wlo")
        s_used = sem("s_used")
        s_acc = sem("s_acc")
        s_zero = sem("s_zero")
        s_cst = sem("s_cst")
        s_xt = sem("s_xt")
        s_xd = sem("s_xd")
        s_xa = sem("s_xa")
        s_hi = sem("s_hi")
        s_lo = sem("s_lo")
        s_sq = sem("s_sq")
        s_add = sem("s_add")
        s_nst = sem("s_nst")
        s_nms = sem("s_nms")
        s_nrc = sem("s_nrc")
        s_nbc = sem("s_nbc")
        s_rB = sem("s_rB")
        s_mix = sem("s_mix")
        s_r = sem("s_r")
        s_ahi = sem("s_ahi")
        s_alo = sem("s_alo")
        s_lam = sem("s_lam")
        s_ksq = sem("s_ksq")
        s_ksum = sem("s_ksum")
        s_kms = sem("s_kms")
        s_krs = sem("s_krs")
        s_kn = sem("s_kn")
        s_kT = sem("s_kT")
        s_kg = sem("s_kg")
        s_qsq = sem("s_qsq")
        s_qst = sem("s_qst")
        s_qms = sem("s_qms")
        s_qrs = sem("s_qrs")
        s_khi = sem("s_khi")
        s_klo = sem("s_klo")
        s_qhi = sem("s_qhi")
        s_qlo = sem("s_qlo")
        s_vhi = sem("s_vhi")
        s_vlo = sem("s_vlo")
        s_S = sem("s_S")
        s_mx = sem("s_mx")
        s_exp = sem("s_exp")
        s_sc = sem("s_sc")
        s_at = sem("s_at")
        s_T = sem("s_T")
        s_Thi = sem("s_Thi")
        s_Tlo = sem("s_Tlo")
        s_pv = sem("s_pv")
        s_oc = sem("s_oc")
        s_ost = sem("s_ost")
        s_oms = sem("s_oms")
        s_ors = sem("s_ors")
        s_obc = sem("s_obc")
        s_on = sem("s_on")
        s_fT = sem("s_fT")
        s_fc = sem("s_fc")
        s_out = sem("s_out")

        win_d = a_w_in.rearrange("l (k p) c -> p (l k) c", p=P)
        wout_d = a_w_out.rearrange("l (k p) c -> p (l k) c", p=P)
        wkv_d = w_kv.rearrange("(k p) c -> p k c", p=P)
        wq_d = w_q.rearrange("l (k p) c -> p (l k) c", p=P)
        wo_d = w_o.rearrange("l (k p) c -> p (l k) c", p=P)
        up_d = [w_up[l].rearrange("(k p) c -> p k c", p=P) for l in range(2)]
        dn_d = [w_down[l].rearrange("(k p) c -> p k c", p=P) for l in range(2)]
        out_d = out.rearrange("b (t p) d -> p (b t) d", p=P)
        x_d = x.rearrange("b (t p) d -> p (b t) d", p=P)

        block = ctx.enter_context(nc.Block())

        @block.sync
        def _(sp):
            def load(n, src, off=0):
                if n >= RAW:
                    sp.wait_ge(s_wlo, off + n - RAW + 1)
                dst = w_raw[:, n % RAW, :].rearrange("p (k c) -> p k c", k=src.shape[1])
                sp.dma_start(dst, src).then_inc(s_raw[n % RAW], 16)

            def small(dst, src):
                sp.dma_start(dst, src).then_inc(s_par, 16)

            def cols(w, c):
                return w[:, :, c * P:(c + 1) * P]

            def load_x(t):
                sp.dma_start(x_tok[:, t, :], x_d[:, t, :]).then_inc(s_x[t], 16)

            for t in range(TB - 1):
                load_x(t)
            for j in range(KC):
                for i, part in enumerate((1, 2, 0)):
                    load(S_IN + 3 * j + i, cols(win_d, part * KC + j))
                    if j == 0 and i == 0:
                        load_x(TB - 1)
                    if j == 0 and i == 1:
                        with nc.allow_non_contiguous_dma(reason="conv taps: one float a feature"):
                            sp.dma_start(conv[:, :, :], a_conv.rearrange("l w (k p) -> p (l w) k", p=P)).then_inc(s_conv, 16)
                if j == 2:
                    with nc.allow_non_contiguous_dma(reason="gains: one float a feature"):
                        small(gains[:, g_m0:g_m1 + 1, :], mlp_norm.rearrange("l (k p) -> p l k", p=P))
                        small(gains[:, g_kv, :], kv_norm.rearrange("(k p) -> p k", p=P))
                        small(gains[:, g_b, :], b_norm.rearrange("l (k p) -> p (l k)", p=P))
                if j == 4:
                    with nc.allow_non_contiguous_dma(reason="gains: one float a feature"):
                        for c in range(2):
                            small(hg[c * HD:(c + 1) * HD, 0:1], q_norm.rearrange("l d -> d l"))
                            small(hg[c * HD:(c + 1) * HD, 1:2], k_norm.rearrange("(d o) -> d o", o=1))
                        small(hg[:, 2:3], sub_norm.rearrange("l d -> d l"))
                if j == 6:
                    for i, v in enumerate((lam_q1, lam_k1, lam_q2, lam_k2)):
                        small(lamv[:, i, :], v.to_broadcast([P, HD]))
            for m in range(KC):
                load(S_OUT + m, cols(wout_d, m))

            def mlp(layer, base):
                with sp.Fori(0, NQ) as q:
                    for j in range(8):
                        load(base + j, up_d[layer][:, :, bass.ds(q * D + j * P, P)], q * 16)
                    for m in range(8):
                        load(base + 8 + m, dn_d[layer][:, bass.ds(q * KC, KC), m * P:(m + 1) * P], q * 16)

            mlp(0, S_MLP0)
            for n in range(16):
                g, kk = n // 4, n % 4
                load(S_KV + n, wkv_d[:, 2 * kk:2 * kk + 2, g * T:(g + 1) * T])
            for h in range(H):
                load(S_Q + h, cols(wq_d, h))
            for m in range(KC):
                load(S_WO + m, cols(wo_d, m))
            mlp(1, S_MLP1)
            for m in range(KC):
                sp.wait_ge(s_fc, m + 1)
                sp.dma_start(out_d[:, :, m * P:(m + 1) * P],
                             kv[:, m, :].rearrange("p (t c) -> p t c", t=TB)).then_inc(s_out, 16)
            sp.wait_ge(s_out, 16 * KC)

        @block.gpsimd
        def _(pool):
            nc.gpsimd.memset(ident[:], 0.0).then_inc(s_zero, 1)
            nc.gpsimd.memset(maskb[:], 0.0).then_inc(s_zero, 1)
            pool.wait_ge(s_zero, 2)
            nc.gpsimd.affine_select(out=ident[:], in_=ident[:], compare_op=ALU.not_equal, fill=1.0, base=0,
                                    pattern=[[-1, P]], channel_multiplier=1).then_inc(s_zero, 1)
            nc.gpsimd.affine_select(out=maskb[:], in_=maskb[:], compare_op=ALU.is_ge, fill=NEG, base=0,
                                    pattern=[[-1, P]], channel_multiplier=1).then_inc(s_zero, 1)
            nc.gpsimd.memset(mhalf[:], -0.5).then_inc(s_zero, 1)
            zero = [(t, b, j) for t in (at_hi, at_lo) for b, j in ((0, 1), (1, 3))]

            def norm(i):
                if i > NORM_A:
                    pool.wait_ge(s_nst, i)
                    nc.gpsimd.memset(sqsum, 0.0).then_inc(s_zero, 1)
                    pool.wait_ge(s_zero, 5 + i + (len(zero) if i == NORM_M1 else 0))
                    for m in range(KC):
                        pool.wait_ge(s_sq, 8 * i + m + 1)
                        nc.gpsimd.tensor_tensor(sqsum, sqsum, sqb[m % 2], ALU.add).then_inc(s_add, 1)
                        pool.wait_ge(s_add, 8 * i + m + 1)
                pool.wait_ge(s_nms, i + 1)
                nc.gpsimd.tensor_tensor(rcol[:, i, :], nms[:, i, :], mhalf[:, 0:TB], ALU.pow).then_inc(s_nrc, 1)

            norm(NORM_A)
            norm(NORM_M0)
            norm(NORM_B)

            def make_q_scale(h, b):
                pool.wait_ge(s_qms, h * 2 + 2)
                nc.gpsimd.tensor_tensor(qpw[:], qms[:, b, :], mhalf[:, 0:8], ALU.pow).then_inc(s_qrs, 1)
                pool.wait_ge(s_qrs, h * 2 + 1)
                nc.gpsimd.tensor_tensor(q_scale[:, b, :].rearrange("p (t c) -> p t c", c=2),
                                        qpw[:].rearrange("p (t c) -> p t c", c=2),
                                        rcol[:, NORM_B, :].unsqueeze(2).to_broadcast([P, TB, 2]), ALU.mult).then_inc(s_qrs, 1)

            def out_scale(h):
                pool.wait_ge(s_oms, h + 1)
                nc.gpsimd.tensor_tensor(ors[:], oms[:], mhalf[:, 0:8], ALU.pow).then_inc(s_ors, 1)

            pool.wait_ge(s_alo, 32)
            pool.wait_ge(s_used, S_KV)
            for t, b, j in zero:
                nc.gpsimd.memset(t[b][:, j, 0:P].bitcast(F32), 0.0).then_inc(s_zero, 1)

            def k_lo_part(h, b):
                pool.wait_ge(s_khi, h + 1)
                nc.gpsimd.tensor_tensor(k_lo[b], kv[:, bass.ds(h, 1), :].rearrange("p a b -> p (a b)"), k_hi[b].bitcast(F32),
                                        ALU.subtract).then_inc(s_klo, 1)

            for g in range(2):
                pool.wait_ge(s_kms, g + 1)
                nc.gpsimd.tensor_tensor(k_rs[:, g, :], k_ms[:, g, :], mhalf[:], ALU.pow).then_inc(s_krs, 1)
            for h in range(2):
                k_lo_part(h, h)
            make_q_scale(0, 0)

            def v_split(h):
                pool.wait_ge(s_vhi, h + 1)
                nc.gpsimd.tensor_tensor(v_lo, v_all[:, :, bass.ds(h * P, P)], v_hi.bitcast(F32), ALU.subtract).then_inc(s_vlo, 1)

            def out_lo(h):
                pool.wait_ge(s_hi, h + (8 * I_O + 1))
                nc.gpsimd.tensor_tensor(h2[:, 1, bass.ds(h, 1), :].rearrange("p a b -> p (a b)"), o_sb,
                                        h2[:, 0, bass.ds(h, 1), :].rearrange("p a b -> p (a b)").bitcast(F32),
                                        ALU.subtract).then_inc(s_lo, 1)

            def head(h, b, prev, nxt, far):
                if nxt is not None:
                    if prev is not None:
                        k_lo_part(nxt, 1 - b)
                    make_q_scale(nxt, 1 - b)
                v_split(h)
                if prev is not None:
                    out_scale(prev)
                    out_lo(prev)

            heads(pool, head)
            out_scale(H - 1)
            out_lo(H - 1)
            norm(NORM_M1)

        @block.tensor
        def _(pe):
            def wait_slab(n, off=0):
                pe.wait_ge(s_wlo, off + n + 1)

            def wait_acc(u, off=0):
                if u >= ACC:
                    pe.wait_ge(s_acc, off + u - ACC + 1)

            def product(bank, n, src, ks, wait_chunk=None):
                s = slot(n)
                for k in ks:
                    if wait_chunk is not None:
                        wait_chunk(k)
                    for i, (w, half) in enumerate(((w_hi, 0), (w_hi, 1), (w_lo, 0))):
                        last = nc.tensor.matmul(ps[:, bank, :], w[:, s, k * P:(k + 1) * P], src(half, k),
                                                start=(k == 0 and i == 0), stop=(k == KC - 1 and i == 2))
                return last

            def operand(i):
                return lambda half, k: h_of[i][:, half, k, :]

            def chunks_of(i):
                return lambda k: pe.wait_ge(s_lo, 8 * i + k + 1)

            def dense(n, u, i, first=False):
                wait_acc(u)
                wait_slab(n)
                product(u % ACC, n, operand(i), range(KC), chunks_of(i) if first else None).then_inc(s_used, 1)

            def norm_sums(i):
                pe.wait_ge(s_add, 8 * (i + 1))
                for t in range(TB):
                    last = nc.tensor.matmul(ps[:, STAT, 2 * t:2 * t + 2], sqsum[:, t * P:(t + 1) * P], ones2[:],
                                            start=True, stop=True)
                last.then_inc(s_nst, 1)

            def spread(bank, col, done):
                for t in range(TB):
                    last = nc.tensor.matmul(ps[:, bank, t * P:(t + 1) * P], col(t), ident[:], start=True, stop=True)
                last.then_inc(done, 1)

            def norm_spread(i):
                pe.wait_ge(s_nrc, i + 1)
                spread(BC, lambda t: rcol[:, i, t:t + 1].to_broadcast([P, P]), s_nbc)

            pe.wait_ge(s_zero, 5)
            pe.wait_ge(s_cst, 5)
            for t in range(TB):
                pe.wait_ge(s_x[t], 16)
                for hf in range(2):
                    for k in range(4):
                        c = (4 * hf + k) * P
                        last = nc.tensor.transpose(ps[:, 2 * t + hf, k * P:(k + 1) * P], x_tok[:, t, c:c + P], ident[:])
                    last.then_inc(s_xt, 1)
            pe.wait_ge(s_xd, TB - 1)
            pe.wait_ge(s_xa, TB + 1)

            for n in range(N_IN):
                dense(S_IN + n, U_IN + n, I_A, n == 0)
                if n == 1:
                    norm_sums(NORM_A)
                if n == 2:
                    norm_spread(NORM_A)
            for m in range(KC):
                dense(S_OUT + m, U_OUT + m, I_Z, m == 0)

            def mlp(layer, base, ubase, inp, norm):
                def quarter(q, first=False, last=False):
                    for j in range(8):
                        wait_acc(ubase + j, q * 16)
                        wait_slab(base + j, q * 16)
                        product((ubase + j) % ACC, base + j, operand(inp), range(KC),
                                chunks_of(inp) if first and j == 0 else None).then_inc(s_used, 1)
                        if first and j == 0:
                            norm_sums(norm)
                        if first and j == 1:
                            norm_spread(norm)
                    for m in range(8):
                        wait_acc(ubase + 8 + m, q * 16)
                        wait_slab(base + 8 + m, q * 16)

                        def act_chunk(k):
                            pe.wait_ge(s_alo, q * 8 + (32 * layer + k + 1))
                        product((ubase + m) % ACC, base + 8 + m, lambda half, k: ah[:, 8 * half + k, :],
                                range(KC), act_chunk if m == 0 else None).then_inc(s_used, 1)
                        if last and layer == 1 and m >= 1:
                            final(m - 1)
                    if last and layer == 1:
                        final(KC - 1)

                quarter(0, first=True)
                with pe.Fori(1, NQ - 1) as q:
                    quarter(q)
                quarter(NQ - 1, last=True)

            def final(m):
                pe.wait_ge(s_acc, U_MLP1 + 16 * (NQ - 1) + 8 + m + 1)
                if m >= 2:
                    pe.wait_ge(s_fc, m - 1)
                for t in range(TB):
                    last = nc.tensor.transpose(ps[:, BC + m % 2, t * P:(t + 1) * P], xT[:, m, t * P:(t + 1) * P], ident[:])
                last.then_inc(s_fT, 1)

            mlp(0, S_MLP0, U_MLP0, I_M0, NORM_M0)

            def transpose_k(h):
                pe.wait_ge(s_kn, TB * (h // 4 + 1))
                if h >= 2:
                    pe.wait_ge(s_kg, h - 1)
                for t in range(TB):
                    last = nc.tensor.transpose(ps[:, BC + h % 2, t * P:(t + 1) * P],
                                               kv[:, h, t * P:(t + 1) * P], ident[:])
                last.then_inc(s_kT, 1)

            for n in range(16):
                g, kk = n // 4, n % 4
                wait_slab(S_KV + n)
                s = slot(S_KV + n)
                for t in range(TB):
                    use = 4 * g + t
                    if kk == 0:
                        if use < ACC:
                            wait_acc(U_KV + use)
                        elif use >= KV_BANKS:
                            pe.wait_ge(s_acc, U_KV + use - KV_BANKS + 1)
                    for k2 in range(2):
                        k = 2 * kk + k2
                        if g == 0 and t == 0:
                            pe.wait_ge(s_lo, 8 * I_KV + k + 1)
                        for i, (half, w) in enumerate(((0, w_hi), (0, w_lo), (1, w_hi))):
                            last = nc.tensor.matmul(ps[:, use % KV_BANKS, :], h2[:, half, k, t * P:(t + 1) * P],
                                                    w[:, s, k2 * T:(k2 + 1) * T],
                                                    start=(k == 0 and i == 0), stop=(k == KC - 1 and i == 2))
                last.then_inc(s_used, 1)
                if n == 0:
                    norm_sums(NORM_B)
                if K_T_AFTER <= n < K_T_AFTER + H:
                    transpose_k(n - K_T_AFTER)

            def head_sums(h, sq, bank, at):
                pe.wait_ge(s_qsq, h + 1)
                if not at_start(h):
                    pe.wait_ge(s_qms, h * 2)
                for t in range(TB):
                    last = nc.tensor.matmul(ps[:, bank, at + 2 * t:at + 2 * t + 2], sq[:, t * P:(t + 1) * P], comp2[:],
                                            start=True, stop=True)
                last.then_inc(s_qst, 1)

            def scores(h, i, b):
                if i == 0:
                    pe.wait_ge(s_klo, h + 1)
                    pe.wait_ge(s_qlo, h + 1)
                if not (at_start(h) and i < 2):
                    pe.wait_ge(s_exp, h * 8 + 2 * (i - 1))
                kw = max((i + 1) * P, 2 * P)
                for j, (q, k) in enumerate(((q_hi, k_hi), (q_hi, k_lo), (q_lo, k_hi))):
                    for c in range(2):
                        rows = slice(c * HD, (c + 1) * HD)
                        nc.tensor.matmul(ps[:, 2 * (i % 2) + c, 0:kw], q[b][rows, i * P:(i + 1) * P], k[b][rows, 0:kw],
                                         start=(j == 0), stop=False)
                for c in range(2):
                    last = nc.tensor.matmul(ps[:, 2 * (i % 2) + c, i * P:(i + 1) * P], identb[:], maskb[:], start=False, stop=True)
                last.then_inc(s_S, 1)

            def weights_T(h, i):
                pe.wait_ge(s_at, h * 4 + i + 1)
                if not (at_start(h) and i == 0):
                    pe.wait_ge(s_Thi, h * 4 + i)
                    pe.wait_ge(s_Tlo, h * 4 + i)
                for j in range(i + 1):
                    last = nc.tensor.transpose(ps[:, B_AT, j * P:(j + 1) * P], p_buf[i % 2][:, 0, j * P:(j + 1) * P], ident[:])
                last.then_inc(s_T, 1)

            def values(h, p):
                pe.wait_ge(s_Thi, h * 4 + 2 * p + 2)
                pe.wait_ge(s_Tlo, h * 4 + 2 * p + 2)
                if p == 0:
                    pe.wait_ge(s_vlo, h + 1)
                    if not at_start(h):
                        pe.wait_ge(s_oc, h * 2)
                nj = 2 * p + 2
                for j in range(nj):
                    for i, (v, a) in enumerate(((v_hi, at_hi), (v_hi, at_lo), (v_lo, at_hi))):
                        last = nc.tensor.matmul(ps[:, B_O, p * 256:(p + 1) * 256], v[:, j, :], a[p][:, j, :],
                                                start=(j == 0 and i == 0), stop=(j == nj - 1 and i == 2))
                last.then_inc(s_pv, 1)

            def out_sums(h):
                pe.wait_ge(s_oc, h * 2 + 2)
                for t in range(TB):
                    last = nc.tensor.matmul(ps[:, B_BC, 2 * t:2 * t + 2], o_sq[:, t * P:(t + 1) * P], ones2[:],
                                            start=True, stop=True)
                last.then_inc(s_ost, 1)

            def out_spread(h):
                pe.wait_ge(s_ors, h + 1)
                spread(B_BC, lambda t: ors[:, 2 * t:2 * t + 1].to_broadcast([P, P]), s_obc)

            def project(h, b, ks):
                if 0 in ks:
                    pe.wait_ge(s_wlo, h + (S_Q + 1))
                    pe.wait_ge(s_qlo, h)
                    pe.wait_ge(s_qsq, h)
                return product(B_Q, S_Q + b, operand(I_Q), ks)

            def project_out(m, bank, ks):
                if 0 in ks:
                    wait_slab(S_WO + m)
                return product(bank, S_WO + m, operand(I_O), ks, chunks_of(I_O))

            def head(h, b, prev, nxt, far):
                scores(h, 2, b)
                if nxt is not None:
                    if prev is not None:
                        pe.wait_ge(s_on, prev)
                    head_sums(nxt, sq_q[1 if prev is None else 0], B_BC, 8)
                if far is not None:
                    project(far, b, range(0, 3))
                elif nxt is not None:
                    pe.wait_ge(s_qlo, H)
                    pe.wait_ge(s_qsq, H)
                    project_out(0, B_Q, range(0, 1))
                else:
                    project_out(0, B_Q, range(3, 5))
                if prev is not None:
                    values(prev, 1)
                weights_T(h, 0)
                scores(h, 3, b)
                if far is not None:
                    project(far, b, range(3, 6))
                elif nxt is not None:
                    project_out(0, B_Q, range(1, 2))
                else:
                    project_out(0, B_Q, range(5, 6))
                if prev is not None:
                    pe.wait_ge(s_on, prev)
                    if nxt is not None:
                        pe.wait_ge(s_qms, nxt * 2 + 1)
                    out_sums(prev)
                weights_T(h, 1)
                if nxt is not None:
                    scores(nxt, 0, 1 - b)
                else:
                    pe.wait_ge(s_exp, h * 8 + 6)
                    project_out(1, 1, range(0, 4))
                if far is not None:
                    project(far, b, range(6, KC)).then_inc(s_used, 1)
                elif nxt is not None:
                    project_out(0, B_Q, range(2, 3))
                values(h, 0)
                weights_T(h, 2)
                if nxt is not None:
                    scores(nxt, 1, 1 - b)
                else:
                    project_out(1, 1, range(4, 6))
                if prev is not None:
                    out_spread(prev)
                weights_T(h, 3)

            def first_q(h, ks):
                return product(Q_BANK[h], S_Q + h, operand(I_Q), ks, chunks_of(I_Q) if h == 0 else None)

            pe.wait_ge(s_acc, U_WO - 6)
            wait_slab(S_Q)
            first_q(0, range(KC)).then_inc(s_used, 1)
            wait_slab(S_Q + 1)
            first_q(1, range(0, 3))
            head_sums(0, sq_q[0], STAT, 0)
            first_q(1, range(3, 5))
            pe.wait_ge(s_acc, U_WO)
            scores(0, 0, 0)
            scores(0, 1, 0)
            first_q(1, range(5, KC)).then_inc(s_used, 1)
            heads(pe, head)
            pe.wait_ge(s_exp, 8 * H)
            project_out(2, 2, range(0, 3))
            values(H - 1, 1)
            project_out(1, 1, range(6, 7))
            project_out(0, B_Q, range(6, 7))
            pe.wait_ge(s_on, H - 1)
            out_sums(H - 1)
            for m in range(2, ACC):
                wait_acc(U_WO + m)
                project_out(m, m, range(3 if m == 2 else 0, 7))
                if m == 2:
                    out_spread(H - 1)
            for m in range(ACC):
                project_out(m, WO_BANK[m], range(7, 8)).then_inc(s_used, 1)
            for m in range(ACC, KC):
                if m > ACC:
                    wait_acc(U_WO + m)
                wait_slab(S_WO + m)
                product(WO_BANK[m], S_WO + m, operand(I_O), range(KC)).then_inc(s_used, 1)
            mlp(1, S_MLP1, U_MLP1, I_M1, NORM_M1)

        @block.scalar
        def _(act):
            with nc.allow_non_contiguous_dma(reason="gains: one float a feature"):
                act.dma_start(gains[:, g_a, :], a_norm.rearrange("l (k p) -> p (l k)", p=P)).then_inc(s_gain_a, 16)

            def split(n, off=0):
                act.wait_ge(s_raw[n % RAW], off * (16 // RAW) + 16 * (n // RAW + 1))
                if freed(n):
                    act.wait_ge(s_used, off + freed(n))
                nc.scalar.activation(w_hi[:, slot(n), :], w_raw[:, n % RAW, :], ACT.Copy).then_inc(s_whi, 1)

            def chunk_hi(i, m, g):
                nc.scalar.activation(h_of[i][:, 0, m, :], xT[:, m, :], ACT.Copy, scale=gains[:, g, m:m + 1]).then_inc(s_hi, 1)

            def square(i, m):
                if 8 * i + m >= 2:
                    act.wait_ge(s_add, 8 * i + m - 1)
                nc.scalar.activation(sqb[m % 2], xT[:, m, :], ACT.Square).then_inc(s_sq, 1)

            def row_scales(count):
                act.wait_ge(s_nbc, count)
                nc.scalar.activation(rB[:], ps[:, BC, :], ACT.Copy).then_inc(s_rB, 1)

            for t in range(TB):
                if t == TB - 1:
                    split(0)
                    act.wait_ge(s_xt, 2 * t + 1)
                    nc.scalar.activation(xT[:, 0:4, t * P:(t + 1) * P],
                                         ps[:, 2 * t, :].rearrange("p (k q) -> p k q", k=4), ACT.Copy).then_inc(s_xa, 1)
                act.wait_ge(s_xt, 2 * t + 2)
                nc.scalar.activation(xT[:, 4:8, t * P:(t + 1) * P],
                                     ps[:, 2 * t + 1, :].rearrange("p (k q) -> p k q", k=4), ACT.Copy).then_inc(s_xa, 1)
            act.wait_ge(s_gain_a, 16)
            act.wait_ge(s_xd, TB - 1)
            act.wait_ge(s_xa, TB + 1)
            for m in range(KC):
                chunk_hi(I_A, m, g_a)
                if m == 5:
                    split(1)
            for m in range(KC):
                square(NORM_A, m)
            for n in range(N_IN):
                split(n + AHEAD)
                if n == 2:
                    row_scales(1)
                if n % 3 == 2:
                    j = n // 3
                    act.wait_ge(s_mix, 9 * (j + 1))
                    nc.scalar.activation(h2[:, 0, j, :], mix[5 + j % 2], ACT.Copy).then_inc(s_hi, 1)
            for m in range(KC):
                split(S_OUT + m + AHEAD)
                act.wait_ge(s_acc, U_OUT + m + 1)
                if m == 0:
                    act.wait_ge(s_par, 16 * N_PAR)
                chunk_hi(I_M0, m, g_m0)
                square(NORM_M0, m)

            def mlp(layer, base, ubase, count, after):
                def quarter(q, first=False, last=False):
                    for j in range(8):
                        split(base + j + AHEAD, q * 16)
                        if first and j == 1:
                            row_scales(count)
                        for jj in ((0, 1) if j == 1 else () if j == 0 else (j,)):
                            act.wait_ge(s_r, q * 8 + (32 * layer + jj + 1))
                            nc.scalar.activation(ah[:, jj, :], mix[jj % 2], ACT.Square).then_inc(s_ahi, 1)
                    for m in range(8):
                        n = base + 8 + m + AHEAD
                        if not (last and n + q * 16 >= S_END):
                            split(n, q * 16)
                        if last:
                            after(m)

                quarter(0, first=True)
                with act.Fori(1, NQ - 1) as q:
                    quarter(q)
                quarter(NQ - 1, last=True)

            def after0(m):
                act.wait_ge(s_acc, U_MLP0 + 56 + m + 1)
                chunk_hi(I_KV, m, g_kv)
                square(NORM_B, m)

            mlp(0, S_MLP0, U_MLP0, 2, after0)
            for n in range(16):
                split(S_KV + n + AHEAD)
                if n < KC:
                    chunk_hi(I_Q, n, g_b)
                if n == 1:
                    act.wait_ge(s_cst, 7)
                    nc.scalar.activation(lams[:, 2:4], lams[:, 0:2], ACT.Exp).then_inc(s_lam, 1)
                if n in (4, 8):
                    g = n // 4 - 1
                    for t in range(TB):
                        act.wait_ge(s_acc, U_KV + 4 * g + t + 1)
                        if 4 * g + t >= 2:
                            act.wait_ge(s_ksum, 4 * g + t - 1)
                        nc.scalar.activation(k_sq[t % 2].rearrange("p (h d) -> p h d", h=4), k_tok[g][t],
                                             ACT.Square).then_inc(s_ksq, 1)
                if n > K_T_AFTER:
                    h = n - K_T_AFTER - 1
                    if h == 0:
                        act.wait_ge(s_cst, 12)
                    act.wait_ge(s_kT, h + 1)
                    nc.scalar.activation(kv[:, h, :], ps[:, BC + h % 2, :], ACT.Copy, scale=hgs[:, 1:2]).then_inc(s_kg, 1)

            def k_hi_part(h, b):
                nc.scalar.activation(k_hi[b], kv[:, bass.ds(h, 1), :].rearrange("p a b -> p (a b)"), ACT.Copy).then_inc(s_khi, 1)

            def take_q(h, b, bank, sq):
                nc.scalar.activation(q_hi[b], ps[:, bank, :], ACT.Copy, scale=hgs[:, 0:1]).then_inc(s_qhi, 1)
                nc.scalar.activation(sq, ps[:, bank, :], ACT.Square).then_inc(s_qsq, 1)

            act.wait_ge(s_kg, H)
            act.wait_ge(s_kT, H)
            for h in range(2):
                k_hi_part(h, h)
            act.wait_ge(s_used, S_Q + 1)
            take_q(0, 0, Q_BANK[0], sq_q[0])
            split(S_Q + 2)

            def exps(h, i, b):
                act.wait_ge(s_mx, h * 8 + 2 * i + 2)
                if not (at_start(h) and i < 2):
                    act.wait_ge(s_T, h * 4 + i - 1)
                kw = (i + 1) * P
                for c in range(2):
                    nc.scalar.activation(p_buf[i % 2][:, c, 0:kw], ps[:, 2 * (i % 2) + c, 0:kw], ACT.Exp,
                                         bias=bias[:, i % 2, c:c + 1], scale=q_scale[:, b, 2 * i + c:2 * i + c + 1],
                                         accum_out=rsum[:, i % 2, c:c + 1]).then_inc(s_exp, 1)

            def weights_hi(h, i):
                act.wait_ge(s_T, h * 4 + i + 1)
                if not at_start(h):
                    act.wait_ge(s_pv, h * 2 + i // 2 - 1)
                nc.scalar.activation(at_hi[i // 2][:, 0:i + 1, (i % 2) * P:(i % 2 + 1) * P],
                                     ps[:, B_AT, 0:(i + 1) * P].rearrange("p (j q) -> p j q", j=i + 1), ACT.Copy).then_inc(s_Thi, 1)

            def v_split(h):
                if not at_start(h):
                    act.wait_ge(s_pv, h * 2)
                nc.scalar.activation(v_hi, v_all[:, :, bass.ds(h * P, P)], ACT.Copy).then_inc(s_vhi, 1)

            def copy_o(h):
                act.wait_ge(s_pv, h * 2 + 2)
                if at_start(h):
                    act.wait_ge(s_qst, 2)
                else:
                    act.wait_ge(s_hi, h + 8 * I_O)
                    act.wait_ge(s_lo, h + 8 * I_O)
                    act.wait_ge(s_ost, h)
                nc.scalar.activation(o_sb, ps[:, B_O, :], ACT.Copy).then_inc(s_oc, 1)
                nc.scalar.activation(o_sq, ps[:, B_O, :], ACT.Square).then_inc(s_oc, 1)

            def out_hi(h):
                act.wait_ge(s_on, h + 1)
                nc.scalar.activation(h2[:, 0, bass.ds(h, 1), :].rearrange("p a b -> p (a b)"), o_sb, ACT.Copy).then_inc(s_hi, 1)

            def next_slab(h, b):
                n = S_Q + HEAD_AHEAD + 1 + b
                off = h - b
                act.wait_ge(s_raw[n % RAW], off * 8 + 16 * (n // RAW + 1))
                act.wait_ge(s_used, off + n - 1)
                nc.scalar.activation(w_hi[:, n % 2, :], w_raw[:, n % RAW, :], ACT.Copy).then_inc(s_whi, 1)

            def head(h, b, prev, nxt, far):
                exps(h, 1, b)
                if prev is not None and nxt is not None:
                    k_hi_part(nxt, 1 - b)
                if nxt is not None:
                    next_slab(h, b)
                else:
                    split(S_WO + 2)
                if prev is not None:
                    copy_o(prev)
                weights_hi(h, 0)
                exps(h, 2, b)
                v_split(h)
                weights_hi(h, 1)
                exps(h, 3, b)
                weights_hi(h, 2)
                if nxt is not None:
                    exps(nxt, 0, 1 - b)
                else:
                    split(S_WO + 3)
                if far is not None:
                    act.wait_ge(s_used, far + (S_Q + 1))
                    act.wait_ge(s_qst, far)
                    take_q(far, b, B_Q, sq_q[0])
                weights_hi(h, 3)
                if prev is not None:
                    out_hi(prev)

            exps(0, 0, 0)
            act.wait_ge(s_used, S_Q + 2)
            take_q(1, 1, Q_BANK[1], sq_q[1])
            heads(act, head)
            copy_o(H - 1)
            out_hi(H - 1)

            for m in range(KC):
                for n in WO_SPLITS[m]:
                    split(S_WO + n)
                act.wait_ge(s_acc, U_WO + m + 1)
                chunk_hi(I_M1, m, g_m1)
                square(NORM_M1, m)
            for n in WO_SPLITS[KC]:
                split(S_WO + n)

            def after1(m):
                if m >= 1:
                    copy_out(m - 1)

            def copy_out(m):
                act.wait_ge(s_fT, m + 1)
                nc.scalar.activation(kv[:, m, :], ps[:, BC + m % 2, :], ACT.Copy).then_inc(s_fc, 1)

            mlp(1, S_MLP1, U_MLP1, 3, after1)
            copy_out(KC - 1)

        @block.vector
        def _(dve):
            V = nc.vector
            mixed = [0]

            def mix_step(ins):
                mixed[0] += 1
                ins.then_inc(s_mix, 1)
                dve.wait_ge(s_mix, mixed[0])

            def split(n, off=0):
                dve.wait_ge(s_whi, off + n + 1)
                V.tensor_tensor(w_lo[:, slot(n), :], w_raw[:, n % RAW, :], w_hi[:, slot(n), :].bitcast(F32),
                                ALU.subtract).then_inc(s_wlo, 1)

            def chunk_lo(i, m, g):
                dve.wait_ge(s_hi, 8 * i + m + 1)
                V.scalar_tensor_tensor(h_of[i][:, 1, m, :], xT[:, m, :], gains[:, g, m:m + 1],
                                       h_of[i][:, 0, m, :].bitcast(F32), ALU.mult, ALU.subtract).then_inc(s_lo, 1)

            def residual(n, bank, m, off=0):
                dve.wait_ge(s_used, off + n + 1)
                V.tensor_tensor(xT[:, m, :], ps[:, bank, :], xT[:, m, :], ALU.add).then_inc(s_acc, 1)

            def mean_squares(i):
                dve.wait_ge(s_nst, i + 1)
                V.tensor_scalar(nms[:, i, :], ps[:, STAT, 0:2 * TB].rearrange("p (t c) -> p t c", c=2)[:, :, 0], 1.0 / D, EPS,
                                ALU.mult, ALU.add).then_inc(s_nms, 1)

            V.memset(ones2[:], 1.0).then_inc(s_cst, 1)
            V.memset(comp2[:], 0.0).then_inc(s_cst, 1)
            dve.wait_ge(s_cst, 2)
            V.memset(comp2[0:HD, 0:1], 1.0).then_inc(s_cst, 1)
            V.memset(comp2[HD:P, 1:2], 1.0).then_inc(s_cst, 1)
            V.memset(mix[2][:, 0:2], 0.0).then_inc(s_mix, 1)
            mixed[0] += 1
            dve.wait_ge(s_zero, 3)
            V.tensor_copy(identb[:], ident[:]).then_inc(s_cst, 1)
            for t in range(TB - 1):
                dve.wait_ge(s_xt, 2 * t + 1)
                V.tensor_copy(xT[:, 0:4, t * P:(t + 1) * P],
                              ps[:, 2 * t, :].rearrange("p (k q) -> p k q", k=4)).then_inc(s_xd, 1)
            split(0)
            dve.wait_ge(s_gain_a, 16)
            dve.wait_ge(s_xd, TB - 1)
            dve.wait_ge(s_xa, TB + 1)
            for m in range(KC):
                chunk_lo(I_A, m, g_a)
                if m == 5:
                    split(1)
            for m in range(KC):
                dve.wait_ge(s_sq, m + 1)
                if m == 0:
                    V.tensor_copy(sqsum, sqb[0]).then_inc(s_add, 1)
                else:
                    V.tensor_tensor(sqsum, sqsum, sqb[m % 2], ALU.add).then_inc(s_add, 1)
                dve.wait_ge(s_add, m + 1)

            cr, u, t0, br = mix[0], work[:, U0:U0 + T + 2], mix[1], mix[4]
            for n in range(N_IN):
                if n == 0:
                    split(AHEAD)
                    mean_squares(NORM_A)
                    split(1 + AHEAD)
                    split(2 + AHEAD)
                    dve.wait_ge(s_rB, 1)
                    dve.wait_ge(s_conv, 16)
                elif n > 2:
                    split(n + AHEAD)
                j = n // 3
                acc = ps[:, (U_IN + n) % ACC, :]
                dve.wait_ge(s_used, n + 1)
                if n % 3 == 0:
                    V.tensor_tensor(cr, acc, rB[:], ALU.mult).then_inc(s_acc, 1)
                    dve.wait_ge(s_acc, n + 1)
                    mix_step(V.tensor_tensor(cr, cr, rB[:], ALU.mult))
                elif n % 3 == 1:
                    V.tensor_tensor(u[:, 2:T + 2], acc, cr, ALU.mult).then_inc(s_acc, 1)
                    dve.wait_ge(s_acc, n + 1)
                    mix_step(V.tensor_scalar(t0, u[:, 0:T], conv[:, 0, j:j + 1], None, ALU.mult))
                    mix_step(V.scalar_tensor_tensor(t0, u[:, 1:T + 1], conv[:, 1, j:j + 1], t0, ALU.mult, ALU.add))
                    mix_step(V.scalar_tensor_tensor(t0, u[:, 2:T + 2], conv[:, 2, j:j + 1], t0, ALU.mult, ALU.add))
                else:
                    V.tensor_tensor(br, acc, rB[:], ALU.mult).then_inc(s_acc, 1)
                    dve.wait_ge(s_acc, n + 1)
                    if j >= 2:
                        dve.wait_ge(s_hi, 8 * I_Z + j - 1)
                    z = mix[5 + j % 2]
                    V.tensor_tensor(z, br, t0, ALU.mult).then_inc(s_mix, 9 * (j + 1) - mixed[0])
                    mixed[0] = 9 * (j + 1)
                    dve.wait_ge(s_mix, mixed[0])
                    dve.wait_ge(s_hi, 8 * I_Z + j + 1)
                    V.tensor_tensor(h2[:, 1, j, :], z, h2[:, 0, j, :].bitcast(F32), ALU.subtract).then_inc(s_lo, 1)
            for m in range(KC):
                split(S_OUT + m + AHEAD)
                residual(S_OUT + m, (U_OUT + m) % ACC, m)
                dve.wait_ge(s_acc, U_OUT + m + 1)
                if m == 0:
                    dve.wait_ge(s_par, 16 * N_PAR)
                chunk_lo(I_M0, m, g_m0)

            def mlp(layer, base, ubase, norm, scales, after):
                def unit(j, q):
                    c = 32 * layer + j + 1
                    dve.wait_ge(s_used, q * 16 + base + j + 1)
                    if not (at_start(q) and layer == 0 and j < 2):
                        dve.wait_ge(s_ahi, q * 8 + c - 2)
                    V.scalar_tensor_tensor(mix[j % 2], ps[:, (ubase + j) % ACC, :], 0.0, rB[:], ALU.max, ALU.mult).then_inc(s_r, 1)
                    dve.wait_ge(s_r, q * 8 + c)
                    V.tensor_tensor(mix[2], mix[j % 2], mix[j % 2], ALU.mult).then_inc(s_acc, 1)
                    dve.wait_ge(s_acc, q * 16 + ubase + j + 1)
                    dve.wait_ge(s_ahi, q * 8 + c)
                    V.tensor_tensor(ah[:, 8 + j, :], mix[2], ah[:, j, :].bitcast(F32), ALU.subtract).then_inc(s_alo, 1)

                def quarter(q, first=False, last=False):
                    for j in range(8):
                        split(base + j + AHEAD, q * 16)
                        if first and j == 0:
                            mean_squares(norm)
                        if first and j == 1:
                            dve.wait_ge(s_rB, scales)
                        for jj in ((0, 1) if j == 1 else () if j == 0 else (j,)):
                            unit(jj, q)
                    for m in range(8):
                        n = base + 8 + m
                        if not (last and n + AHEAD + q * 16 >= S_END):
                            split(n + AHEAD, q * 16)
                        residual(n, (ubase + 8 + m) % ACC, m, q * 16)
                        if last:
                            after(m)

                quarter(0, first=True)
                with dve.Fori(1, NQ - 1) as q:
                    quarter(q)
                quarter(NQ - 1, last=True)

            def after0(m):
                dve.wait_ge(s_acc, U_MLP0 + 56 + m + 1)
                chunk_lo(I_KV, m, g_kv)

            mlp(0, S_MLP0, U_MLP0, NORM_M0, 2, after0)

            def lambda_and_gains():
                for i in range(2):
                    V.tensor_tensor_reduce(out=lamp[:], in0=lamv[:, 2 * i, :], in1=lamv[:, 2 * i + 1, :], scale=1.0, scalar=0.0,
                                           op0=ALU.mult, op1=ALU.add, accum_out=lams[:, i:i + 1]).then_inc(s_cst, 1)
                    dve.wait_ge(s_cst, 6 + i)
                for i, c in enumerate((HD ** -0.5, 1.0, 1.0 - LAM_INIT)):
                    V.tensor_scalar(hgs[:, i:i + 1], hg[:, i:i + 1], c, None, ALU.mult).then_inc(s_cst, 1)
                dve.wait_ge(s_lam, 1)
                V.tensor_tensor(lams[:, 4:5], lams[:, 3:4], lams[:, 2:3], ALU.subtract).then_inc(s_cst, 1)
                dve.wait_ge(s_cst, 11)
                V.tensor_scalar(lams[:, 5:6], lams[:, 4:5], -LAM_INIT, None, ALU.add).then_inc(s_cst, 1)

            for n in range(16):
                split(S_KV + n + AHEAD)
                if n == 0:
                    mean_squares(NORM_B)
                if n < KC:
                    chunk_lo(I_Q, n, g_b)
                if n == 1:
                    lambda_and_gains()
                if n in (4, 8):
                    g = n // 4 - 1
                    for t in range(TB):
                        dve.wait_ge(s_ksq, 4 * g + t + 1)
                        V.tensor_reduce(k_ms[:, g, t * 8:(t + 1) * 8], k_sq[t % 2].rearrange("p (c d) -> p c d", d=HD),
                                        AX_X, ALU.add).then_inc(s_ksum, 1)
                    dve.wait_ge(s_ksum, 4 * (g + 1))
                    V.tensor_scalar(k_ms[:, g, :], k_ms[:, g, :], 1.0 / HD, EPS, ALU.mult, ALU.add).then_inc(s_kms, 1)
                if n in (6, 10):
                    g = (n - 6) // 4
                    dve.wait_ge(s_krs, g + 1)
                    for t in range(TB):
                        k_heads = k_tok[g][t].rearrange("p h (c d) -> p h c d", d=HD)
                        scale = k_rs[:, g, t * 8:(t + 1) * 8].rearrange("p (h c) -> p h c", c=2)
                        V.tensor_tensor(k_heads, k_heads, scale.unsqueeze(3).to_broadcast([P, 4, 2, HD]),
                                        ALU.mult).then_inc(s_kn, 1)
                if n % 4 == 3:
                    g = n // 4
                    dve.wait_ge(s_nrc, NORM_B + 1)
                    dve.wait_ge(s_used, S_KV + n + 1)
                    for t in range(TB):
                        to, bank = v_all[:, t, (g - 2) * T:(g - 1) * T], ps[:, (4 * g + t) % KV_BANKS, :]
                        if g < 2:
                            to, bank = k_tok[g][t], bank.rearrange("p (h d) -> p h d", h=4)
                        V.tensor_scalar(to, bank, rcol[:, NORM_B, t:t + 1], None,
                                        ALU.mult).then_inc(s_acc, 1)
            V.scalar_tensor_tensor(r2[:], rcol[:, NORM_B, :], 1.0 / HD, rcol[:, NORM_B, :], ALU.mult, ALU.mult).then_inc(s_cst, 1)
            dve.wait_ge(s_cst, 13)

            def head_ms(h, b, bank, at):
                dve.wait_ge(s_qst, h + 1)
                if not (isinstance(h, int) and h < 2):
                    dve.wait_ge(s_qrs, h * 2 - 3)
                V.tensor_tensor(qms[:, b, :].rearrange("p (t c) -> p t c", c=2),
                                ps[:, bank, at:at + 8].rearrange("p (t c) -> p t c", c=2),
                                r2[:].unsqueeze(2).to_broadcast([P, TB, 2]), ALU.mult).then_inc(s_qms, 1)
                dve.wait_ge(s_qms, h * 2 + 1)
                V.tensor_scalar(qms[:, b, :], qms[:, b, :], EPS, None, ALU.add).then_inc(s_qms, 1)

            def q_lo_part(h, b, bank):
                dve.wait_ge(s_qhi, h + 1)
                dve.wait_ge(s_qsq, h + 1)
                V.scalar_tensor_tensor(q_lo[b], ps[:, bank, :], hgs[:, 0:1], q_hi[b].bitcast(F32),
                                       ALU.mult, ALU.subtract).then_inc(s_qlo, 1)

            q_lo_part(0, 0, Q_BANK[0])
            split(S_Q + 2)
            head_ms(0, 0, STAT, 0)

            def row_max(h, i, hb):
                b = i % 2
                kw = (i + 1) * P
                if i == 0:
                    dve.wait_ge(s_qrs, h * 2 + 2)
                dve.wait_ge(s_S, h * 4 + i + 1)
                if not (at_start(h) and i < 2):
                    dve.wait_ge(s_exp, h * 8 + 2 * i - 2)
                V.tensor_reduce(nmax[:, b, :], ps[:, 2 * b:2 * b + 2, 0:kw], AX_X, ALU.max, negate=True).then_inc(s_mx, 1)
                dve.wait_ge(s_mx, h * 8 + 2 * i + 1)
                V.tensor_tensor(bias[:, b, :], nmax[:, b, :], q_scale[:, hb, 2 * i:2 * i + 2], ALU.mult).then_inc(s_mx, 1)

            def weights(h, i):
                b = i % 2
                kw = (i + 1) * P
                p1, p2 = p_buf[b][:, 0, 0:kw], p_buf[b][:, 1, 0:kw]
                dve.wait_ge(s_exp, h * 8 + 2 * i + 2)
                V.reciprocal(rinv[:, b, :], rsum[:, b, :]).then_inc(s_sc, 1)
                dve.wait_ge(s_sc, h * 8 + 2 * i + 1)
                V.tensor_scalar(p2, p2, rinv[:, b, 1:2], lams[:, 5:6], ALU.mult, ALU.mult).then_inc(s_sc, 1)
                dve.wait_ge(s_sc, h * 8 + 2 * i + 2)
                V.scalar_tensor_tensor(p1, p1, rinv[:, b, 0:1], p2, ALU.mult, ALU.add).then_inc(s_at, 1)

            def weights_lo(h, i):
                dve.wait_ge(s_Thi, h * 4 + i + 1)
                cols = slice((i % 2) * P, (i % 2 + 1) * P)
                V.tensor_tensor(at_lo[i // 2][:, 0:i + 1, cols], ps[:, B_AT, 0:(i + 1) * P].rearrange("p (j q) -> p j q", j=i + 1),
                                at_hi[i // 2][:, 0:i + 1, cols].bitcast(F32), ALU.subtract).then_inc(s_Tlo, 1)

            def out_ms(h):
                dve.wait_ge(s_ost, h + 1)
                if not at_start(h):
                    dve.wait_ge(s_ors, h)
                V.tensor_scalar(oms[:], ps[:, B_BC, 0:8], 1.0 / P, EPS, ALU.mult, ALU.add).then_inc(s_oms, 1)

            def out_norm(h):
                dve.wait_ge(s_obc, h + 1)
                V.scalar_tensor_tensor(o_sb, o_sb, hgs[:, 2:3], ps[:, B_BC, :], ALU.mult, ALU.mult).then_inc(s_on, 1)

            def next_slab(h, b):
                n = S_Q + HEAD_AHEAD + 1 + b
                dve.wait_ge(s_whi, h + (n - b + 1))
                V.tensor_tensor(w_lo[:, n % 2, :], w_raw[:, n % RAW, :], w_hi[:, n % 2, :].bitcast(F32),
                                ALU.subtract).then_inc(s_wlo, 1)

            def head(h, b, prev, nxt, far):
                row_max(h, 2, b)
                if nxt is not None:
                    head_ms(nxt, 1 - b, B_BC, 8)
                if nxt is not None:
                    next_slab(h, b)
                else:
                    split(S_WO + 2)
                weights(h, 1)
                weights_lo(h, 0)
                row_max(h, 3, b)
                weights(h, 2)
                weights_lo(h, 1)
                if prev is not None:
                    out_ms(prev)
                if nxt is not None:
                    row_max(nxt, 0, 1 - b)
                weights(h, 3)
                weights_lo(h, 2)
                if nxt is not None:
                    row_max(nxt, 1, 1 - b)
                if prev is not None:
                    out_norm(prev)
                if far is not None:
                    q_lo_part(far, b, B_Q)
                if nxt is not None:
                    weights(nxt, 0)
                else:
                    split(S_WO + 3)
                weights_lo(h, 3)

            row_max(0, 0, 0)
            row_max(0, 1, 0)
            q_lo_part(1, 1, Q_BANK[1])
            weights(0, 0)
            heads(dve, head)
            out_ms(H - 1)
            out_norm(H - 1)

            for m in range(KC):
                for n in WO_SPLITS[m]:
                    split(S_WO + n)
                residual(S_WO + m, WO_BANK[m], m)
                dve.wait_ge(s_acc, U_WO + m + 1)
                chunk_lo(I_M1, m, g_m1)
            for n in WO_SPLITS[KC]:
                split(S_WO + n)
            mlp(1, S_MLP1, U_MLP1, NORM_M1, 3, lambda m: None)


_INS = ["x", "a_norm", "a_w_in", "a_conv", "a_w_out", "kv_norm", "w_kv", "k_norm", "b_norm", "w_q", "q_norm",
        "lam_q1", "lam_k1", "lam_q2", "lam_k2", "sub_norm", "w_o", "mlp_norm", "w_up", "w_down"]


def kernel(**inputs):
    import numpy as np
    import concourse.bacc as bacc
    from concourse.bass_utils import run_bass_kernel_spmd

    nc = bacc.Bacc("TRN2", target_bir_lowering=False, num_devices=1)
    arrays, args = {}, []
    for name in _INS:
        a = np.ascontiguousarray(inputs[name])
        arrays[f"in_{name}"] = a
        args.append(nc.dram_tensor(f"in_{name}", a.shape, mybir.dt.from_np(a.dtype), kind="ExternalInput").ap())
    out = nc.dram_tensor("out_x", (1, T, D), F32, kind="ExternalOutput").ap()
    build(nc, *args, out)
    r = run_bass_kernel_spmd(nc, [arrays], core_ids=[0])
    return r.results[0]["out_x"]
```
